# Optimizing a Trainium2 kernel written in Bass

```python
import math, functools
import jax, jax.numpy as jnp
from jax import lax
import numpy as np

D_MODEL = 1024
BATCH = 1
SEQ = 512
DEPTH = 1

ATT_HEADS = 8
ATT_HEAD_DIM = 64
ATT_WIDTH = ATT_HEADS * ATT_HEAD_DIM
ATT_PATTERNS = ((128, 1), (512, 4), (2048, 16))
ATT_BLOCK = 128
SSD_HEADS = 8
SSD_HEAD_DIM = 64
SSD_WIDTH = SSD_HEADS * SSD_HEAD_DIM
SSD_GROUPS = 2
SSD_STATE = 128
SSD_CHUNK = 128
SSD_CONV_CH = SSD_WIDTH + 2 * SSD_GROUPS * SSD_STATE
DT_MIN = 0.001
DT_MAX = 0.1
LRU_WIDTH = 512
LRU_BLOCKS = 8
LRU_BLOCK_W = LRU_WIDTH // LRU_BLOCKS
LRU_C = 8.0
CONV_WIDTH = 4
D_MIX = ATT_WIDTH + SSD_WIDTH + LRU_WIDTH
IN_COLS = 3 * ATT_WIDTH + SSD_WIDTH + SSD_CONV_CH + SSD_HEADS + 2 * LRU_WIDTH
D_FF = ((8 * D_MODEL + 3 * 256 - 1) // (3 * 256)) * 256
NORM_EPS = 1e-6
SSD_NORM_EPS = 1e-5


def rmsnorm(x, g, eps=NORM_EPS):
    xf = x.astype(jnp.float32)
    y = xf * lax.rsqrt(jnp.mean(xf * xf, axis=-1, keepdims=True) + eps)
    return (y * g.astype(jnp.float32)).astype(x.dtype)

def causal_depthwise_conv(x, w, b):
    k_width, s = w.shape[0], x.shape[1]
    xp = jnp.pad(x, ((0, 0), (k_width - 1, 0), (0, 0)))
    y = b + xp[:, k_width - 1:] * w[k_width - 1]
    for k in range(k_width - 1):
        y = y + xp[:, k:k + s] * w[k]
    return y

def split_cols(proj):
    sizes = (ATT_WIDTH, ATT_WIDTH, ATT_WIDTH, SSD_WIDTH, SSD_CONV_CH, SSD_HEADS, LRU_WIDTH, LRU_WIDTH)
    offsets = np.cumsum(sizes)[:-1].tolist()
    return jnp.split(proj, offsets, axis=-1)

def dilated_branch(q, k, v, window, dilation, slopes):
    b, s, h, dh = q.shape
    length = s // dilation
    nb = -(-length // ATT_BLOCK)
    pad = nb * ATT_BLOCK - length

    def to_blocks(t):
        t = t.reshape(b, length, dilation, h, dh).transpose(0, 2, 3, 1, 4)
        t = jnp.pad(t, ((0, 0), (0, 0), (0, 0), (0, pad), (0, 0)))
        return t.reshape(b, dilation, h, nb, ATT_BLOCK, dh)

    def with_prev(t):
        prev = jnp.pad(t[:, :, :, :-1], ((0, 0), (0, 0), (0, 0), (1, 0), (0, 0), (0, 0)))
        return jnp.concatenate([prev, t], axis=4)

    qb, kb, vb = to_blocks(q), to_blocks(k), to_blocks(v)
    kk, vv = with_prev(kb), with_prev(vb)
    scores = jnp.einsum('brhnqd,brhnkd->brhnqk', qb, kk,
                        preferred_element_type=jnp.float32) * (ATT_HEAD_DIM ** -0.5)
    qi = jnp.arange(ATT_BLOCK)[:, None]
    ki = jnp.arange(2 * ATT_BLOCK)[None, :]
    dist = ATT_BLOCK + qi - ki
    band = (dist >= 0) & (dist <= window // dilation)
    valid = band[None] & ((jnp.arange(nb)[:, None, None] > 0) | (ki[None] >= ATT_BLOCK))
    alibi = -slopes[:, None, None] * (dilation * dist).astype(jnp.float32)
    scores = scores + alibi[None, None, :, None]
    scores = jnp.where(valid[None, None, None], scores, -jnp.inf)
    m = jnp.max(scores, axis=-1)
    p = jnp.exp(scores - m[..., None])
    den = jnp.sum(p, axis=-1)
    num = jnp.einsum('brhnqk,brhnkd->brhnqd', p, vv.astype(jnp.float32))

    def from_blocks(t):
        t = t.reshape(b, dilation, h, nb * ATT_BLOCK, *t.shape[5:])[:, :, :, :length]
        t = jnp.moveaxis(t, 3, 1)
        return t.reshape(b, s, h, *t.shape[4:])

    return from_blocks(num), from_blocks(m), from_blocks(den)

def dilated_attention(q, k, v):
    b, s, _ = q.shape
    shp = (b, s, ATT_HEADS, ATT_HEAD_DIM)
    q, k, v = q.reshape(shp), k.reshape(shp), v.reshape(shp)
    slopes = jnp.exp2(-8.0 * jnp.arange(1, ATT_HEADS + 1, dtype=jnp.float32) / ATT_HEADS)
    branches = [dilated_branch(q, k, v, w, d, slopes) for (w, d) in ATT_PATTERNS]
    m_all = functools.reduce(jnp.maximum, [br[1] for br in branches])
    num = jnp.zeros(shp, jnp.float32)
    den = jnp.zeros(shp[:3], jnp.float32)
    for n_g, m_g, d_g in branches:
        e = jnp.exp(m_g - m_all)
        num = num + n_g * e[..., None]
        den = den + d_g * e
    return (num / den[..., None]).reshape(b, s, ATT_WIDTH)

def ssd_chunked_scan(x, dt, a, bm, cm):
    b, s, h, p = x.shape
    n = bm.shape[-1]
    q = SSD_CHUNK
    nc = s // q
    rep = h // bm.shape[2]
    x = x.reshape(b, nc, q, h, p)
    dt = dt.reshape(b, nc, q, h)
    bh = jnp.repeat(bm, rep, axis=2).reshape(b, nc, q, h, n)
    ch = jnp.repeat(cm, rep, axis=2).reshape(b, nc, q, h, n)
    acs = jnp.cumsum(dt * a, axis=2)
    seg = acs[:, :, :, None, :] - acs[:, :, None, :, :]
    causal = jnp.tril(jnp.ones((q, q), dtype=bool))[None, None, :, :, None]
    lmat = jnp.exp(jnp.where(causal, seg, -jnp.inf))
    scores = jnp.einsum('bcihn,bcjhn->bcijh', ch, bh) * lmat * dt[:, :, None, :, :]
    y_diag = jnp.einsum('bcijh,bcjhp->bcihp', scores, x)
    decay_to_end = jnp.exp(acs[:, :, -1:, :] - acs)
    states = jnp.einsum('bcjhn,bcjh,bcjhp->bchpn', bh, decay_to_end * dt, x)
    chunk_decay = jnp.exp(acs[:, :, -1, :])

    def step(carry, inp):
        st, dc = inp
        return dc[:, :, None, None] * carry + st, carry

    _, prev = lax.scan(step, jnp.zeros((b, h, p, n), x.dtype),
                       (jnp.moveaxis(states, 1, 0), jnp.moveaxis(chunk_decay, 1, 0)))
    prev = jnp.moveaxis(prev, 0, 1)
    y_off = jnp.einsum('bcihn,bchpn,bcih->bcihp', ch, prev, jnp.exp(acs))
    return (y_diag + y_off).reshape(b, s, h, p)

def ssd_mixer(z, xbc, dt_raw, conv_w, conv_b, dt_bias, a_log, d_skip, norm_w):
    b, s, _ = z.shape
    f32 = jnp.float32
    xbc = jax.nn.silu(causal_depthwise_conv(xbc, conv_w, conv_b)).astype(f32)
    xs, bm, cm = jnp.split(xbc, [SSD_WIDTH, SSD_WIDTH + SSD_GROUPS * SSD_STATE], axis=-1)
    xs = xs.reshape(b, s, SSD_HEADS, SSD_HEAD_DIM)
    bm = bm.reshape(b, s, SSD_GROUPS, SSD_STATE)
    cm = cm.reshape(b, s, SSD_GROUPS, SSD_STATE)
    dt = jax.nn.softplus(dt_raw.astype(f32) + dt_bias.astype(f32))
    a = -jnp.exp(a_log.astype(f32))
    y = ssd_chunked_scan(xs, dt, a, bm, cm) + d_skip.astype(f32)[:, None] * xs
    y = y.reshape(b, s, SSD_WIDTH) * jax.nn.silu(z.astype(f32))
    yg = y.reshape(b, s, SSD_GROUPS, SSD_WIDTH // SSD_GROUPS)
    yg = yg * lax.rsqrt(jnp.mean(yg * yg, axis=-1, keepdims=True) + SSD_NORM_EPS)
    return yg.reshape(b, s, SSD_WIDTH) * norm_w.astype(f32)

def rglru_mixer(gate_in, x_in, conv_w, conv_b, wa, ba, wx, bx, lam):
    b, s, _ = x_in.shape
    f32 = jnp.float32
    gate = jax.nn.gelu(gate_in.astype(f32))
    xc = causal_depthwise_conv(x_in, conv_w, conv_b).astype(f32)
    xb = xc.reshape(b, s, LRU_BLOCKS, LRU_BLOCK_W)
    r = jax.nn.sigmoid(jnp.einsum('bsnc,ncd->bsnd', xb, wa.astype(f32)).reshape(b, s, LRU_WIDTH) + ba.astype(f32))
    i = jax.nn.sigmoid(jnp.einsum('bsnc,ncd->bsnd', xb, wx.astype(f32)).reshape(b, s, LRU_WIDTH) + bx.astype(f32))
    log_a = -LRU_C * r * jax.nn.softplus(-lam.astype(f32))
    a = jnp.exp(log_a)
    u = jnp.sqrt(-jnp.expm1(2.0 * log_a)) * (i * xc)

    def combine(left, right):
        a_l, h_l = left
        a_r, h_r = right
        return a_l * a_r, a_r * h_l + h_r

    _, h = lax.associative_scan(combine, (a, u), axis=1)
    return h * gate

def swiglu(h, w_gate, w_up, w_down):
    return (jax.nn.silu(h @ w_gate) * (h @ w_up)) @ w_down

def hybrid_layer(x, norm_mix, w_in, ssd_conv_w, ssd_conv_b, ssd_dt_bias, ssd_a_log, ssd_d, ssd_norm,
                 lru_conv_w, lru_conv_b, lru_wa, lru_ba, lru_wx, lru_bx, lru_lambda, w_out,
                 norm_ffn, w_gate, w_up, w_down):
    h = rmsnorm(x, norm_mix)
    q, k, v, z, xbc, dt_raw, g_lru, x_lru = split_cols(h @ w_in)
    att = dilated_attention(q, k, v).astype(x.dtype)
    ssd = ssd_mixer(z, xbc, dt_raw, ssd_conv_w, ssd_conv_b, ssd_dt_bias, ssd_a_log, ssd_d, ssd_norm).astype(x.dtype)
    lru = rglru_mixer(g_lru, x_lru, lru_conv_w, lru_conv_b, lru_wa, lru_ba, lru_wx, lru_bx, lru_lambda).astype(x.dtype)
    x = x + jnp.concatenate([att, ssd, lru], axis=-1) @ w_out
    x = x + swiglu(rmsnorm(x, norm_ffn), w_gate, w_up, w_down)
    return x

def first_inputs(seed: int = 0) -> dict:
    key = jax.random.key(seed)
    ks = jax.random.split(key, 24)
    f32 = jnp.float32
    L = DEPTH

    def nrm(k, shape, scale):
        return scale * jax.random.normal(k, shape, f32)

    x = nrm(ks[0], (BATCH, SEQ, D_MODEL), 1.0)
    norm_mix = 1.0 + nrm(ks[1], (L, D_MODEL), 0.05)
    w_in = nrm(ks[2], (L, D_MODEL, IN_COLS), D_MODEL ** -0.5)
    ssd_conv_w = nrm(ks[3], (L, CONV_WIDTH, SSD_CONV_CH), CONV_WIDTH ** -0.5)
    ssd_conv_b = nrm(ks[4], (L, SSD_CONV_CH), 0.02)
    dt0 = jnp.exp(jax.random.uniform(ks[5], (L, SSD_HEADS), f32, math.log(DT_MIN), math.log(DT_MAX)))
    ssd_dt_bias = dt0 + jnp.log(-jnp.expm1(-dt0))
    ssd_a_log = jnp.log(jax.random.uniform(ks[6], (L, SSD_HEADS), f32, 1.0, 16.0))
    ssd_d = 1.0 + nrm(ks[7], (L, SSD_HEADS), 0.1)
    ssd_norm = 1.0 + nrm(ks[8], (L, SSD_WIDTH), 0.05)
    lru_conv_w = nrm(ks[9], (L, CONV_WIDTH, LRU_WIDTH), CONV_WIDTH ** -0.5)
    lru_conv_b = nrm(ks[10], (L, LRU_WIDTH), 0.02)
    lru_wa = nrm(ks[11], (L, LRU_BLOCKS, LRU_BLOCK_W, LRU_BLOCK_W), LRU_BLOCK_W ** -0.5)
    lru_ba = nrm(ks[12], (L, LRU_WIDTH), 0.02)
    lru_wx = nrm(ks[13], (L, LRU_BLOCKS, LRU_BLOCK_W, LRU_BLOCK_W), LRU_BLOCK_W ** -0.5)
    lru_bx = nrm(ks[14], (L, LRU_WIDTH), 0.02)
    a_c = jax.random.uniform(ks[15], (L, LRU_WIDTH), f32, 0.9, 0.999)
    a_base = a_c ** (1.0 / LRU_C)
    lru_lambda = jnp.log(a_base) - jnp.log1p(-a_base)
    w_out = nrm(ks[16], (L, D_MIX, D_MODEL), D_MIX ** -0.5)
    norm_ffn = 1.0 + nrm(ks[17], (L, D_MODEL), 0.05)
    w_gate = nrm(ks[18], (L, D_MODEL, D_FF), D_MODEL ** -0.5)
    w_up = nrm(ks[19], (L, D_MODEL, D_FF), D_MODEL ** -0.5)
    w_down = nrm(ks[20], (L, D_FF, D_MODEL), D_FF ** -0.5)
    norm_final = 1.0 + nrm(ks[21], (D_MODEL,), 0.05)
    return {'x': x, 'norm_mix': norm_mix, 'w_in': w_in, 'ssd_conv_w': ssd_conv_w, 'ssd_conv_b': ssd_conv_b,
            'ssd_dt_bias': ssd_dt_bias, 'ssd_a_log': ssd_a_log, 'ssd_d': ssd_d, 'ssd_norm': ssd_norm,
            'lru_conv_w': lru_conv_w, 'lru_conv_b': lru_conv_b, 'lru_wa': lru_wa, 'lru_ba': lru_ba,
            'lru_wx': lru_wx, 'lru_bx': lru_bx, 'lru_lambda': lru_lambda, 'w_out': w_out,
            'norm_ffn': norm_ffn, 'w_gate': w_gate, 'w_up': w_up, 'w_down': w_down, 'norm_final': norm_final}

def first_block(x, norm_mix, w_in, ssd_conv_w, ssd_conv_b, ssd_dt_bias, ssd_a_log, ssd_d, ssd_norm,
              lru_conv_w, lru_conv_b, lru_wa, lru_ba, lru_wx, lru_bx, lru_lambda, w_out,
              norm_ffn, w_gate, w_up, w_down, norm_final):
    for l in range(DEPTH):
        x = hybrid_layer(x, norm_mix[l], w_in[l], ssd_conv_w[l], ssd_conv_b[l], ssd_dt_bias[l], ssd_a_log[l],
                         ssd_d[l], ssd_norm[l], lru_conv_w[l], lru_conv_b[l], lru_wa[l], lru_ba[l],
                         lru_wx[l], lru_bx[l], lru_lambda[l], w_out[l], norm_ffn[l], w_gate[l], w_up[l], w_down[l])
    return rmsnorm(x, norm_final)


DEPTH_2 = 2

NSA_HEADS = 8
NSA_HEAD_DIM = 64
NSA_KV_HEADS = 2
NSA_GROUP = NSA_HEADS // NSA_KV_HEADS
NSA_WIDTH = NSA_HEADS * NSA_HEAD_DIM
KV_WIDTH = NSA_KV_HEADS * NSA_HEAD_DIM
CMP_LEN = 32
CMP_STRIDE = 16
CMP_HIDDEN = 256
SLC_LEN = 64
SLC_TOPN = 16
WINDOW = 512
Q_BLOCK = 128
RET_HEADS = 4
RET_HEAD_DIM = 128
RET_WIDTH = RET_HEADS * RET_HEAD_DIM
RET_CHUNK = 128
MEM_LEN = 256
MEM_HEADS = 4
MEM_HEAD_DIM = D_MODEL // MEM_HEADS
D_FF_2 = 2816
EPS = 1e-6
NEG = -1e30

IN_SIZES = (NSA_WIDTH,
            KV_WIDTH, KV_WIDTH,
            KV_WIDTH, KV_WIDTH,
            KV_WIDTH, KV_WIDTH,
            NSA_HEADS * 3,
            RET_WIDTH, RET_WIDTH, RET_WIDTH, RET_WIDTH)
IN_WIDTH = sum(IN_SIZES)
IN_OFFSETS = tuple(int(o) for o in np.cumsum(IN_SIZES)[:-1])


def rms_norm(x, g):
    xf = x.astype(jnp.float32)
    y = xf * lax.rsqrt(jnp.mean(xf * xf, axis=-1, keepdims=True) + EPS)
    return (y * g.astype(jnp.float32)).astype(x.dtype)

def swiglu_2(x, w_gate, w_up, w_down):
    return (jax.nn.silu(x @ w_gate) * (x @ w_up)) @ w_down

def masked_softmax(s, mask):
    s = jnp.where(mask, s, NEG)
    m = jnp.max(s, axis=-1, keepdims=True)
    p = jnp.where(mask, jnp.exp(s - m), 0.0)
    return p / jnp.maximum(jnp.sum(p, axis=-1, keepdims=True), 1e-30)

def alibi_slopes(n):
    return jnp.asarray(2.0 ** (-8.0 * np.arange(1, n + 1) / n), dtype=jnp.float32)

def compress(kv, pe, w1, w2):
    B, T, G, dh = kv.shape
    nc = (T - CMP_LEN) // CMP_STRIDE + 1
    idx = np.arange(nc)[:, None] * CMP_STRIDE + np.arange(CMP_LEN)[None, :]
    blocks = kv[:, idx] + pe[None, None, :, None, :]
    flat = blocks.transpose(0, 1, 3, 2, 4).reshape(B, nc, G, CMP_LEN * dh)
    return jax.nn.silu(flat @ w1) @ w2

def nsa_mixer(q, k_cmp, v_cmp, k_slc, v_slc, k_win, v_win, gates, cmp_pe, cmp_w1, cmp_w2):
    B, T = q.shape[:2]
    G, R, dh = NSA_KV_HEADS, NSA_GROUP, NSA_HEAD_DIM
    scale = dh ** -0.5
    slopes = alibi_slopes(NSA_HEADS).reshape(G, R)

    kc = compress(k_cmp, cmp_pe[0], cmp_w1[0], cmp_w2[0])
    vc = compress(v_cmp, cmp_pe[1], cmp_w1[1], cmp_w2[1])
    nc = kc.shape[1]
    nsel = T // SLC_LEN
    n_top = min(SLC_TOPN, nsel)

    c_start_np = np.arange(nc) * CMP_STRIDE
    c_end_np = c_start_np + CMP_LEN - 1
    s_start_np = np.arange(nsel) * SLC_LEN
    s_end_np = s_start_np + SLC_LEN - 1
    overlap = jnp.asarray(np.clip(np.minimum(c_end_np[:, None], s_end_np[None, :])
                                  - np.maximum(c_start_np[:, None], s_start_np[None, :]) + 1,
                                  0, None) / CMP_LEN, dtype=jnp.float32)
    c_end = jnp.asarray(c_end_np, dtype=jnp.int32)
    c_mid = jnp.asarray(c_start_np + (CMP_LEN - 1) / 2.0, dtype=jnp.float32)

    k_blocks = k_slc.reshape(B, nsel, SLC_LEN, G, dh).transpose(0, 3, 1, 2, 4)
    v_blocks = v_slc.reshape(B, nsel, SLC_LEN, G, dh).transpose(0, 3, 1, 2, 4)
    k_win_p = jnp.pad(k_win, ((0, 0), (WINDOW, 0), (0, 0), (0, 0)))
    v_win_p = jnp.pad(v_win, ((0, 0), (WINDOW, 0), (0, 0), (0, 0)))

    nb = T // Q_BLOCK
    qb = q.reshape(B, nb, Q_BLOCK, G, R, dh).transpose(1, 0, 2, 3, 4, 5)
    gb = gates.reshape(B, nb, Q_BLOCK, G, R, 3).transpose(1, 0, 2, 3, 4, 5)
    b_ix = jnp.arange(B)[:, None, None, None]
    g_ix = jnp.arange(G)[None, None, :, None]
    jb = jnp.arange(nsel)

    def block_fn(args):
        i, qi, gi = args
        t = i * Q_BLOCK + jnp.arange(Q_BLOCK)
        tf = t.astype(jnp.float32)

        s_c = jnp.einsum('bqgrd,bngd->bgrqn', qi, kc).astype(jnp.float32) * scale
        s_c = s_c - slopes[None, :, :, None, None] * (tf[:, None] - c_mid[None, :])
        p_c = masked_softmax(s_c, (c_end[None, :] <= t[:, None])[None, None, None])
        o_c = jnp.einsum('bgrqn,bngd->bqgrd', p_c.astype(vc.dtype), vc)

        imp = jnp.einsum('bgrqn,nj->bqgj', p_c, overlap)
        cur = t // SLC_LEN
        forced = (jb[None, :] == 0) | (jb[None, :] == cur[:, None]) | (jb[None, :] == cur[:, None] - 1)
        valid = jb[None, :] <= cur[:, None]
        imp = jnp.where(forced[None, :, None, :], 1e4,
                        jnp.where(valid[None, :, None, :], imp, -1.0))
        _, idx = lax.top_k(imp, n_top)

        ks = k_blocks[b_ix, g_ix, idx].reshape(B, Q_BLOCK, G, n_top * SLC_LEN, dh)
        vs = v_blocks[b_ix, g_ix, idx].reshape(B, Q_BLOCK, G, n_top * SLC_LEN, dh)
        spos = (idx[..., None] * SLC_LEN + jnp.arange(SLC_LEN)).reshape(B, Q_BLOCK, G, 1, n_top * SLC_LEN)
        dist_s = t[None, :, None, None, None] - spos
        s_s = jnp.einsum('bqgrd,bqgmd->bqgrm', qi, ks).astype(jnp.float32) * scale
        s_s = s_s - slopes[None, None, :, :, None] * dist_s.astype(jnp.float32)
        p_s = masked_softmax(s_s, dist_s >= 0)
        o_s = jnp.einsum('bqgrm,bqgmd->bqgrd', p_s.astype(vs.dtype), vs)

        kw = lax.dynamic_slice_in_dim(k_win_p, i * Q_BLOCK, WINDOW + Q_BLOCK, axis=1)
        vw = lax.dynamic_slice_in_dim(v_win_p, i * Q_BLOCK, WINDOW + Q_BLOCK, axis=1)
        kpos = i * Q_BLOCK - WINDOW + jnp.arange(WINDOW + Q_BLOCK)
        dist_w = t[:, None] - kpos[None, :]
        mask_w = (dist_w >= 0) & (dist_w < WINDOW) & (kpos[None, :] >= 0)
        s_w = jnp.einsum('bqgrd,bkgd->bqgrk', qi, kw).astype(jnp.float32) * scale
        s_w = s_w - slopes[None, None, :, :, None] * dist_w[None, :, None, None, :].astype(jnp.float32)
        p_w = masked_softmax(s_w, mask_w[None, :, None, None, :])
        o_w = jnp.einsum('bqgrk,bkgd->bqgrd', p_w.astype(vw.dtype), vw)

        gs = jax.nn.sigmoid(gi.astype(jnp.float32))
        o = (gs[..., 0:1] * o_c.astype(jnp.float32) + gs[..., 1:2] * o_s.astype(jnp.float32)
             + gs[..., 2:3] * o_w.astype(jnp.float32))
        return o.reshape(B, Q_BLOCK, NSA_WIDTH).astype(q.dtype)

    out = lax.map(block_fn, (jnp.arange(nb), qb, gb))
    return out.transpose(1, 0, 2, 3).reshape(B, T, NSA_WIDTH)

def retention(q, k, v, g, gn_gain):
    B, T, Hr, d = q.shape
    C = RET_CHUNK
    nch = T // C
    log_g = jnp.log(1.0 - jnp.exp2(-5.0 - jnp.arange(Hr, dtype=jnp.float32)))
    pos = jnp.arange(C, dtype=jnp.float32)
    diff = pos[:, None] - pos[None, :]
    decay_mask = jnp.where(diff >= 0, jnp.exp(jnp.maximum(diff, 0.0) * log_g[:, None, None]), 0.0)
    q_dec = jnp.exp((pos + 1.0) * log_g[:, None])
    k_dec = jnp.exp((C - 1.0 - pos) * log_g[:, None])
    chunk_dec = jnp.exp(C * log_g)

    def to_chunks(a):
        return a.astype(jnp.float32).reshape(B, nch, C, Hr, d).transpose(1, 0, 3, 2, 4)
    qc, kc, vc = to_chunks(q), to_chunks(k * (d ** -0.5)), to_chunks(v)

    def step(state, xs):
        qi, ki, vi = xs
        s = jnp.einsum('bhnd,bhmd->bhnm', qi, ki) * decay_mask[None]
        inner = jnp.einsum('bhnm,bhmd->bhnd', s, vi)
        cross = jnp.einsum('bhnd,bhde->bhne', qi, state) * q_dec[None, :, :, None]
        new_state = (state * chunk_dec[None, :, None, None]
                     + jnp.einsum('bhmd,bhme->bhde', ki * k_dec[None, :, :, None], vi))
        return new_state, inner + cross

    state0 = jnp.zeros((B, Hr, d, d), jnp.float32)
    _, o = lax.scan(step, state0, (qc, kc, vc))
    o = o.transpose(1, 0, 3, 2, 4).reshape(B, T, Hr, d)
    mu = jnp.mean(o, axis=-1, keepdims=True)
    var = jnp.mean(jnp.square(o - mu), axis=-1, keepdims=True)
    o = (o - mu) * lax.rsqrt(var + EPS) * gn_gain.astype(jnp.float32).reshape(Hr, d)
    o = o.reshape(B, T, RET_WIDTH) * jax.nn.silu(g.astype(jnp.float32))
    return o.astype(q.dtype)

def hybrid_mixer(h, w_in, cmp_pe, cmp_w1, cmp_w2, nsa_out_g, ret_gn_g, w_out):
    B, T, _ = h.shape
    parts = jnp.split(h @ w_in, IN_OFFSETS, axis=-1)
    q_n, kc, vc, ks, vs, kw, vw, gates, q_r, k_r, v_r, g_r = parts
    kvs = lambda a: a.reshape(B, T, NSA_KV_HEADS, NSA_HEAD_DIM)
    o_nsa = nsa_mixer(q_n.reshape(B, T, NSA_HEADS, NSA_HEAD_DIM), kvs(kc), kvs(vc), kvs(ks), kvs(vs),
                      kvs(kw), kvs(vw), gates.reshape(B, T, NSA_HEADS, 3), cmp_pe, cmp_w1, cmp_w2)
    o_nsa = rms_norm(o_nsa, nsa_out_g)
    rs = lambda a: a.reshape(B, T, RET_HEADS, RET_HEAD_DIM)
    o_ret = retention(rs(q_r), rs(k_r), rs(v_r), g_r, ret_gn_g)
    return jnp.concatenate([o_nsa, o_ret], axis=-1) @ w_out

def memory_xattn(h, m, wq, wk, wv, wo):
    B, T, _ = h.shape
    M = m.shape[1]
    q = (h @ wq).reshape(B, T, MEM_HEADS, MEM_HEAD_DIM)
    k = (m @ wk).reshape(B, M, MEM_HEADS, MEM_HEAD_DIM)
    v = (m @ wv).reshape(B, M, MEM_HEADS, MEM_HEAD_DIM)
    s = jnp.einsum('bthd,bmhd->bhtm', q, k).astype(jnp.float32) * (MEM_HEAD_DIM ** -0.5)
    p = jax.nn.softmax(s, axis=-1)
    o = jnp.einsum('bhtm,bmhd->bthd', p.astype(v.dtype), v).reshape(B, T, D_MODEL)
    return o @ wo

def second_inputs(seed: int = 0) -> dict:
    key = jax.random.key(seed)
    ks = jax.random.split(key, 28)
    f32 = jnp.float32

    def dense(k, shape, fan_in):
        return jax.random.normal(k, shape, f32) * (fan_in ** -0.5)

    def gain(k, n):
        return 1.0 + 0.02 * jax.random.normal(k, (DEPTH_2, n), f32)

    L, dh = CMP_LEN, NSA_HEAD_DIM
    return {
        "x": jax.random.normal(ks[0], (BATCH, SEQ, D_MODEL), f32),
        "mem": jax.random.normal(ks[1], (BATCH, MEM_LEN, D_MODEL), f32),
        "ffn1_pre_g": gain(ks[2], D_MODEL),
        "ffn1_w_gate": dense(ks[3], (DEPTH_2, D_MODEL, D_FF_2), D_MODEL),
        "ffn1_w_up": dense(ks[4], (DEPTH_2, D_MODEL, D_FF_2), D_MODEL),
        "ffn1_w_down": dense(ks[5], (DEPTH_2, D_FF_2, D_MODEL), D_FF_2),
        "ffn1_post_g": gain(ks[6], D_MODEL),
        "mix_pre_g": gain(ks[7], D_MODEL),
        "w_in": dense(ks[8], (DEPTH_2, D_MODEL, IN_WIDTH), D_MODEL),
        "cmp_pe": 0.5 * jax.random.normal(ks[9], (DEPTH_2, 2, L, dh), f32),
        "cmp_w1": dense(ks[10], (DEPTH_2, 2, L * dh, CMP_HIDDEN), L * dh),
        "cmp_w2": dense(ks[11], (DEPTH_2, 2, CMP_HIDDEN, dh), CMP_HIDDEN),
        "nsa_out_g": gain(ks[12], NSA_WIDTH),
        "ret_gn_g": gain(ks[13], RET_WIDTH),
        "w_out": dense(ks[14], (DEPTH_2, NSA_WIDTH + RET_WIDTH, D_MODEL), NSA_WIDTH + RET_WIDTH),
        "mix_post_g": gain(ks[15], D_MODEL),
        "xa_pre_g": gain(ks[16], D_MODEL),
        "xa_mem_g": gain(ks[17], D_MODEL),
        "xa_wq": dense(ks[18], (DEPTH_2, D_MODEL, D_MODEL), D_MODEL),
        "xa_wk": dense(ks[19], (DEPTH_2, D_MODEL, D_MODEL), D_MODEL),
        "xa_wv": dense(ks[20], (DEPTH_2, D_MODEL, D_MODEL), D_MODEL),
        "xa_wo": dense(ks[21], (DEPTH_2, D_MODEL, D_MODEL), D_MODEL),
        "xa_post_g": gain(ks[22], D_MODEL),
        "ffn2_pre_g": gain(ks[23], D_MODEL),
        "ffn2_w_gate": dense(ks[24], (DEPTH_2, D_MODEL, D_FF_2), D_MODEL),
        "ffn2_w_up": dense(ks[25], (DEPTH_2, D_MODEL, D_FF_2), D_MODEL),
        "ffn2_w_down": dense(ks[26], (DEPTH_2, D_FF_2, D_MODEL), D_FF_2),
        "ffn2_post_g": gain(ks[27], D_MODEL),
    }

def second_block(x, mem, ffn1_pre_g, ffn1_w_gate, ffn1_w_up, ffn1_w_down, ffn1_post_g,
              mix_pre_g, w_in, cmp_pe, cmp_w1, cmp_w2, nsa_out_g, ret_gn_g, w_out, mix_post_g,
              xa_pre_g, xa_mem_g, xa_wq, xa_wk, xa_wv, xa_wo, xa_post_g,
              ffn2_pre_g, ffn2_w_gate, ffn2_w_up, ffn2_w_down, ffn2_post_g):
    for l in range(DEPTH_2):
        y = swiglu_2(rms_norm(x, ffn1_pre_g[l]), ffn1_w_gate[l], ffn1_w_up[l], ffn1_w_down[l])
        x = x + 0.5 * rms_norm(y, ffn1_post_g[l])
        y = hybrid_mixer(rms_norm(x, mix_pre_g[l]), w_in[l], cmp_pe[l], cmp_w1[l], cmp_w2[l],
                         nsa_out_g[l], ret_gn_g[l], w_out[l])
        x = x + rms_norm(y, mix_post_g[l])
        y = memory_xattn(rms_norm(x, xa_pre_g[l]), rms_norm(mem, xa_mem_g[l]),
                         xa_wq[l], xa_wk[l], xa_wv[l], xa_wo[l])
        x = x + rms_norm(y, xa_post_g[l])
        y = swiglu_2(rms_norm(x, ffn2_pre_g[l]), ffn2_w_gate[l], ffn2_w_up[l], ffn2_w_down[l])
        x = x + 0.5 * rms_norm(y, ffn2_post_g[l])
    return x


def setup_inputs(seed=0):
    out = dict(first_inputs(seed))
    for name, value in second_inputs(seed + 1).items():
        if name != "x":
            out[name + "_2"] = value
    return out


def reference(
    x, norm_mix, w_in, ssd_conv_w, ssd_conv_b, ssd_dt_bias, ssd_a_log, ssd_d, ssd_norm,
    lru_conv_w, lru_conv_b, lru_wa, lru_ba, lru_wx, lru_bx, lru_lambda, w_out, norm_ffn, w_gate,
    w_up, w_down, norm_final, mem_2, ffn1_pre_g_2, ffn1_w_gate_2, ffn1_w_up_2, ffn1_w_down_2,
    ffn1_post_g_2, mix_pre_g_2, w_in_2, cmp_pe_2, cmp_w1_2, cmp_w2_2, nsa_out_g_2, ret_gn_g_2,
    w_out_2, mix_post_g_2, xa_pre_g_2, xa_mem_g_2, xa_wq_2, xa_wk_2, xa_wv_2, xa_wo_2,
    xa_post_g_2, ffn2_pre_g_2, ffn2_w_gate_2, ffn2_w_up_2, ffn2_w_down_2, ffn2_post_g_2,
):
    x = first_block(
        x, norm_mix, w_in, ssd_conv_w, ssd_conv_b, ssd_dt_bias, ssd_a_log, ssd_d, ssd_norm,
        lru_conv_w, lru_conv_b, lru_wa, lru_ba, lru_wx, lru_bx, lru_lambda, w_out, norm_ffn,
        w_gate, w_up, w_down, norm_final,
    )
    return second_block(
        x, mem_2, ffn1_pre_g_2, ffn1_w_gate_2, ffn1_w_up_2, ffn1_w_down_2, ffn1_post_g_2,
        mix_pre_g_2, w_in_2, cmp_pe_2, cmp_w1_2, cmp_w2_2, nsa_out_g_2, ret_gn_g_2, w_out_2,
        mix_post_g_2, xa_pre_g_2, xa_mem_g_2, xa_wq_2, xa_wk_2, xa_wv_2, xa_wo_2, xa_post_g_2,
        ffn2_pre_g_2, ffn2_w_gate_2, ffn2_w_up_2, ffn2_w_down_2, ffn2_post_g_2,
    )


_drawn_inputs = setup_inputs


def setup_inputs(seed=0):
    import zlib

    import numpy as np

    out = dict(_drawn_inputs(seed))
    spreads = {}
    factors = {'lru_ba': 8.0,
     'lru_bx': 8.0,
     'ffn1_pre_g_2': 2.844,
     'ffn1_post_g_2': 4.019,
     'nsa_out_g_2': 3.546,
     'ret_gn_g_2': 6.197,
     'mix_post_g_2': 3.093,
     'xa_pre_g_2': 3.572,
     'xa_post_g_2': 3.376,
     'ffn2_pre_g_2': 5.334,
     'ffn2_post_g_2': 7.38}
    for name, (base, spread) in spreads.items():
        noise = np.random.default_rng([zlib.crc32(name.encode()), seed]).standard_normal(out[name].shape)
        drawn = base * np.exp(spread * noise) if base else spread * noise
        out[name] = __import__('jax').numpy.asarray(drawn.astype(out[name].dtype))
    for name, factor in factors.items():
        out[name] = (out[name] * factor).astype(out[name].dtype)
    return out
```

```python
import math
from contextlib import contextmanager

import numpy as np
import concourse.bass as bass
from concourse import mybir

F32 = mybir.dt.float32
F32R = mybir.dt.float32r
ACT = mybir.ActivationFunctionType
ALU = mybir.AluOpType
AX_X = mybir.AxisListType.X
ET = mybir.EngineType

P = 128
T = 512
TB = T // P
D = 1024
KT = D // P
MEM = 256
CHUNK = 2048
FF = 2816
FT = FF // P
FPAIR = FT // 2
LAYERS = 2
HEADS = 8
DH = 64
NEG = -1e30
EPS = 1e-6
SSD_EPS = 1e-5
MAIN = (mybir.EngineType.PE, mybir.EngineType.Activation, mybir.EngineType.DVE, mybir.EngineType.Pool)

CONST_COLS = {}


def const_table():
    i = np.arange(P)
    parts = []

    def add(name, a):
        CONST_COLS[name] = (sum(p.shape[1] for p in parts), a.shape[1])
        parts.append(a.astype(np.float32))

    add("ident", np.eye(P))
    add("ones", np.ones((P, 1)))
    add("zeros", np.zeros((P, P)))
    add("half_neg", -0.5 * np.ones((P, 16)))
    d = i[:, None] - (np.arange(T)[None, :] - (T - P))
    add("dist", np.where(d >= 0, -d, NEG))
    count = (d <= 128).astype(int) + (d % 4 == 0) + (d % 16 == 0)
    add("lncount", np.where((d >= 0) & (count > 0), np.log(np.maximum(count, 1)), NEG))
    add("tri", (i[:, None] <= i[None, :]) * 1.0)
    add("allones", np.ones((P, P)))
    add("negtri", np.where(i[None, :] >= i[:, None], 0.0, NEG))
    log_g = [math.log(1.0 - 2.0 ** (-5.0 - h)) for h in range(4)]
    diff = i[None, :] - i[:, None]
    add("decay", np.concatenate([np.where(diff >= 0, np.exp(np.maximum(diff, 0) * g), 0.0) for g in log_g], 1))
    add("qdec", np.stack([np.exp((i + 1.0) * g) for g in log_g], 1))
    add("kdec", np.stack([np.exp((P - 1.0 - i) * g) for g in log_g], 1))
    n = np.arange(32)
    t = (np.arange(TB)[:, None, None] * P + i[None, :, None])
    cm = np.where((n * 16 + 31 <= t) & (n < 31), -(t - (n * 16 + 15.5)), NEG)
    add("cmpdist", cm.transpose(1, 0, 2).reshape(P, -1))
    add("rowvalid", (t[:, :, 0] >= 31).T * 1.0)
    return np.concatenate(parts, 1)


CONSTS = const_table()
CHUNK_DEC = [math.exp(P * math.log(1.0 - 2.0 ** (-5.0 - h))) for h in range(4)]
SLOPES = [2.0 ** -(h + 1) for h in range(HEADS)]

PAR1 = {}
PAR2 = {}


def _cols(table, spec):
    at = 0
    for name, n in spec:
        table[name] = (at, n)
        at += n
    return at


NPAR1 = _cols(PAR1, [("norm_mix", 8), ("norm_ffn", 8), ("ssd_conv_w", 32), ("ssd_conv_b", 8), ("dt_bias", 8),
                     ("a_log", 8), ("d", 8), ("ssd_norm", 4), ("lru_conv_w", 16), ("lru_conv_b", 4),
                     ("lru_ba", 4), ("lru_bx", 4), ("lru_lambda", 4), ("norm_final", 8)])
NPAR2 = _cols(PAR2, [("ffn1_pre_g", 8), ("ffn1_post_g", 8), ("mix_pre_g", 8), ("mix_post_g", 8), ("xa_pre_g", 8),
                     ("xa_mem_g", 8), ("xa_post_g", 8), ("ffn2_pre_g", 8), ("ffn2_post_g", 8), ("nsa_out_g", 4),
                     ("ret_gn_g", 4), ("cmp_pe", 32), ("cmp_w2k", 256), ("cmp_w2v", 128)])


class Count:
    def __init__(self, sem, loops):
        self.sem, self.loops, self.value = sem, loops, None


class Before:
    def __init__(self, loop, name):
        self.loop, self.name = loop, name


class Chunks:
    def __init__(self, sem, mul, off):
        self.sem, self.mul, self.off = sem, mul, off


class Item:
    def __init__(self, engine, what, count, inc, loops):
        self.engine, self.what, self.count, self.inc, self.loops = engine, what, count, inc, loops
        self.chunks = 0


class Loop:
    def __init__(self, n):
        self.n, self.items, self.var, self.per, self.names = n, [], None, {}, {}

    def before(self, name):
        return Before(self, name)


class Engine:
    def __init__(self, queue, name, handle):
        self.queue, self.name, self.handle, self.latest = queue, name, handle, None

    def wait(self, *counts):
        for c in counts:
            if isinstance(c, (list, tuple)):
                self.wait(*c)
            elif c is not None:
                self.queue.add(Item(self, c, None, 0, tuple(self.queue.loops)))

    def do(self, fn, signal=True, sem=None, inc=1):
        count = Count(sem or self.name, tuple(self.queue.loops)) if signal else None
        self.queue.add(Item(self, fn, count, inc, tuple(self.queue.loops)))
        if sem is None:
            self.latest = count
        return count


class Queue:
    def __init__(self, nc):
        self.nc, self.items, self.loops, self.sems = nc, [[]], [], {}
        self.PE, self.ACT, self.DVE, self.POOL = (Engine(self, n, e) for n, e in (
            ("pe", nc.tensor), ("act", nc.scalar), ("dve", nc.vector), ("pool", nc.gpsimd)))
        self.engines = (self.PE, self.ACT, self.DVE, self.POOL)

    def add(self, item):
        self.items[-1].append(item)

    def sem(self, name):
        if name not in self.sems:
            self.sems[name] = self.nc.alloc_semaphore("s_" + name)
        return self.sems[name]

    @contextmanager
    def loop(self, n):
        l = Loop(n)
        self.add(l)
        self.items.append(l.items)
        self.loops.append(l)
        yield l
        self.items.pop()
        self.loops.pop()

    def barrier(self):
        reached = [e.latest for e in self.engines if e.latest is not None]
        for e in self.engines:
            e.wait(*reached)

    def number(self, items, at):
        for it in items:
            if isinstance(it, Loop):
                before = dict(at)
                self.number(it.items, at)
                for sem in at:
                    it.per[sem] = at[sem] - before.get(sem, 0)
                    at[sem] += (it.n - 1) * it.per[sem]
            elif it.count is not None:
                at[it.count.sem] = at.get(it.count.sem, 0) + it.inc
                it.count.value = at[it.count.sem]
            else:
                it.chunks = at.get("hi", 0)

    def value(self, wait):
        c, factors = wait.what, {}
        if isinstance(c, Chunks):
            return c.sem, wait.chunks * c.mul + c.off, {l: l.per.get("hi", 0) * c.mul for l in wait.loops}
        back = None
        if isinstance(c, Before):
            back, c = c.loop, c.loop.names[c.name]
        value = c.value
        for l in c.loops:
            per = l.per[c.sem]
            if l is back:
                value -= per
            if l in wait.loops:
                factors[l] = per
            else:
                value += (l.n - 1) * per
        assert value > 0, "a wait's value has to be positive in the first iteration too"
        return c.sem, value, factors

    def emit(self):
        self.final = {}
        self.number(self.items[0], self.final)
        self.emit_items(self.items[0])

    def emit_items(self, items):
        for it in items:
            if isinstance(it, Loop):
                with self.nc.Fori(0, it.n, engines=MAIN) as it.var:
                    self.emit_items(it.items)
            elif callable(it.what):
                ins = it.what()
                if it.count is not None:
                    ins.then_inc(self.sem(it.count.sem), it.inc)
            else:
                sem, value, factors = self.value(it)
                for l, per in factors.items():
                    if per:
                        value = l.var * per + value
                it.engine.handle.wait_ge(self.sem(sem), value)


class Kernel:
    def __init__(self, nc, wstream, xT, memT, consts, par1, lru_w, par2, outT):
        self.nc = nc
        self.g = Queue(nc)
        self.PE, self.ACT, self.DVE, self.POOL = self.g.engines
        self.dram = dict(w=wstream, x=xT, mem=memT, c=consts, p1=par1, lw=lru_w, p2=par2, out=outT)
        self.names = 0
        self.slot = 0
        self.sums_due = []
        self.place_memory()

    def place_memory(self):
        nc = self.nc
        self.top = (nc.sbuf_base + 63) // 64 * 64

        def put(name, cols, dt=F32, at=None):
            t = nc.alloc_sbuf_tensor_at(name, [P, cols], dt, offset=self.top if at is None else at)
            if at is None:
                self.top += (cols * 4 + 63) // 64 * 64
            return t

        self.put = put
        self.raw = [put(f"raw{s}", CHUNK) for s in range(2)]
        self.whi = [put(f"whi{s}", CHUNK, F32R) for s in range(2)]
        self.wlo = [put(f"wlo{s}", CHUNK, F32R) for s in range(2)]
        self.x = put("x", KT * T)
        self.at_h = self.top
        self.hhi = put("hhi", KT * T, F32R)
        self.hlo = put("hlo", KT * T, F32R)
        self.consts = put("consts", CONSTS.shape[1])
        self.par1 = put("par1", NPAR1)
        self.par2 = put("par2", NPAR2)
        self.tmp = [put(f"tmp{n}", T) for n in range(4)]
        self.stat = put("stat", 160)
        self.at_big = self.top
        self.big_end = nc.sbuf_usable_end
        self.bank = [nc.alloc_psum_tensor(f"bank{b}", [P, T], F32) for b in range(8)]
        self.bank_read = [[] for _ in range(8)]

    def arena(self, start, end):
        at = [start]

        def put(name, cols, dt=F32):
            t = self.nc.alloc_sbuf_tensor_at(name, [P, cols], dt, offset=at[0])
            at[0] += (cols * 4 + 31) // 32 * 32
            assert at[0] <= end, (name, at[0] - end)
            return t
        put.at = at
        return put

    def c(self, name, a=0, n=None):
        o, w = CONST_COLS[name]
        return self.consts[:, o + a:o + (w if n is None else a + n)]

    def p1(self, name, a=0, n=1):
        o = PAR1[name][0]
        return self.par1[:, o + a:o + a + n]

    def p2(self, name, a=0, n=1):
        o = PAR2[name][0]
        return self.par2[:, o + a:o + a + n]

    def r(self, a):
        return a() if callable(a) else a

    def act(self, out, in_, func, **kw):
        return self.ACT.do(lambda: self.nc.scalar.activation(self.r(out), self.r(in_), func, **kw))

    def tt(self, out, a, b, op, engine=None):
        e = engine or self.DVE
        return e.do(lambda: e.handle.tensor_tensor(self.r(out), self.r(a), self.r(b), op))

    def ts(self, out, a, s1, op0, s2=None, op1=None):
        if op1 is None:
            return self.DVE.do(lambda: self.nc.vector.tensor_scalar(self.r(out), self.r(a), s1, None, op0))
        return self.DVE.do(lambda: self.nc.vector.tensor_scalar(self.r(out), self.r(a), s1, s2, op0, op1))

    def stt(self, out, a, s, b, op0, op1):
        return self.DVE.do(lambda: self.nc.vector.scalar_tensor_tensor(self.r(out), self.r(a), s, self.r(b), op0, op1))

    def copy(self, out, a):
        return self.DVE.do(lambda: self.nc.vector.tensor_copy(out, a))

    def memset(self, out, value):
        return self.DVE.do(lambda: self.nc.vector.memset(out, value))

    def reciprocal(self, out, a):
        return self.DVE.do(lambda: self.nc.vector.reciprocal(out, a))

    def reduce(self, out, a, op, negate=None):
        return self.DVE.do(lambda: self.nc.vector.tensor_reduce(out, a, AX_X, op, negate=negate))

    def mm(self, out, lhsT, rhs, start, stop, skip=False):
        return self.PE.do(lambda: self.nc.tensor.matmul(out, lhsT, rhs, start=start, stop=stop, skip_group_check=skip),
                          signal=stop)

    def transpose(self, out, in_):
        n = in_.shape[0]
        return self.PE.do(lambda: self.nc.tensor.transpose(out, in_, self.c("ident")[0:n, 0:n]))

    def load(self, out, in_, sem):
        return self.ACT.do(lambda: self.nc.scalar.dma_start(out, self.r(in_)), sem=sem, inc=16)

    def split(self, src, hi, lo, *deps, war=()):
        self.ACT.wait(*deps, *war)
        a = self.act(hi, src, ACT.Copy)
        hif = (lambda: self.r(hi).bitcast(F32))
        self.DVE.wait(a)
        b = self.tt(lo, src, hif, ALU.subtract)
        return [a, b]

    def barrier(self):
        self.g.barrier()
        self.bank_read = [[] for _ in range(8)]

    def split(self, src, hi, lo):
        hi_done = self.act(hi, src, ACT.Copy)
        self.DVE.wait(hi_done)
        lo_done = self.tt(lo, src, lambda: self.r(hi).bitcast(F32), ALU.subtract)
        return [hi_done, lo_done]

    def split_next_chunk(self, slot, products):
        raw, hi, lo = self.raw[slot], self.whi[slot], self.wlo[slot]
        loaded = Chunks(f"raw{slot}", 8, 16 if slot == 0 else 8)
        self.ACT.wait(loaded, products)
        self.ACT.do(lambda: self.nc.scalar.activation(hi[:, :], raw[:, :], ACT.Copy), sem="hi")
        hi_there = Chunks("hi", 1, 0)
        self.POOL.wait(hi_there)
        self.POOL.do(lambda: self.nc.gpsimd.tensor_tensor(lo[:, :], raw[:, :], hi[:, :].bitcast(F32), ALU.subtract), sem="lo")

    def chunk(self, body):
        slot = self.slot
        self.PE.wait(Chunks("hi", 1, -1), Chunks("lo", 1, -1))
        products = yield from body(self.whi[slot], self.wlo[slot])
        self.slot ^= 1
        self.split_next_chunk(slot, products)

    def mm3(self, out, l, r, start, stop, signal=False):
        self.mm(out, l[0], r[0], start, False)
        self.mm(out, l[0], r[1], False, False)
        return self.PE.do(lambda: self.nc.tensor.matmul(out, l[1], r[0], start=False, stop=stop), signal=stop or signal)

    def weights_stationary(self, *args, **kw):
        for _ in self.stationary_steps(*args, **kw):
            pass

    def weights_moving(self, *args, **kw):
        for _ in self.moving_steps(*args, **kw):
            pass

    def stationary_steps(self, banks, acts, nk, evac, k0=0, ktot=None, width=T, ready_k=None):
        ktot = ktot or nk
        part = acts if callable(acts) else (lambda k: [a[:, k * width:(k + 1) * width] for a in acts])

        def body(hi, lo):
            for m in range(2):
                b = banks[m]
                if k0 == 0:
                    self.PE.wait(self.bank_read[b])
                for k in range(nk):
                    ws = [w[:, k * 256 + m * P:k * 256 + m * P + P] for w in (hi, lo)]
                    if ready_k is not None and m == 0:
                        self.PE.wait(ready_k[k0 + k])
                    tile_done = self.mm3(self.bank[b][:, 0:width], ws, part(k0 + k), k0 + k == 0, k0 + k == ktot - 1,
                                         signal=k == nk - 1)
                    if k == 4:
                        self.add_sums_due()
                    if width == T or k % 2:
                        yield
                if k0 + nk == ktot:
                    self.bank_read[b] = [evac(m, b, tile_done)]
            return tile_done
        yield from self.chunk(body)

    def moving_steps(self, acts, c0, n, evac, banks, nblk=TB, width=T, also=None):
        def body(hi, lo):
            if also is not None:
                also(hi, lo)
            for tb in range(nblk):
                b = banks[tb % len(banks)]
                self.PE.wait(self.bank_read[b])
                for k in range(KT):
                    ws = [w[:, k * 256 + c0:k * 256 + c0 + n] for w in (hi, lo)]
                    o = k * width + tb * P
                    tile_done = self.mm3(self.bank[b][:, 0:n], [a[:, o:o + P] for a in acts], ws, k == 0, k == KT - 1)
                    if k % 2:
                        yield
                self.bank_read[b] = [evac(tb, b, tile_done)]
            return tile_done
        yield from self.chunk(body)

    def seed_sums(self, b):
        self.PE.wait(self.bank_read[b])
        z = self.c("zeros")
        self.mm(self.bank[b][:, 0:TB], z[:, 0:P], z[:, 0:TB], True, False, skip=True)

    def add_sums(self, sq, b, nblk=TB):
        for tb in range(nblk):
            o = sq[:, tb * P:(tb + 1) * P]
            added = self.PE.do(lambda tb=tb, o=o: self.nc.tensor.matmul(
                self.bank[b][:, tb:tb + 1], o, self.c("ones"), start=False, stop=True, skip_group_check=True),
                signal=tb == nblk - 1)
        return added

    def sum_later(self, sq, b, squared, note):
        self.sums_due.append((sq, b, squared, note))

    def add_sums_due(self):
        for sq, b, squared, note in self.sums_due:
            self.PE.wait(squared)
            note(self.add_sums(sq, b))
        self.sums_due = []

    def squares_of_x(self, made=None):
        self.seed_sums(0)
        added = []
        for k in range(KT):
            t = self.tmp[k % 2]
            self.ACT.wait(made[k] if made else None, added[k - 2] if k >= 2 else None)
            squared = self.act(t[:, :], self.x[:, k * T:(k + 1) * T], ACT.Square)
            self.PE.wait(squared)
            added.append(self.add_sums(t, 0))
        return added[-1]

    def rstd_rows(self, bs, bb, summed, nblk=TB):
        ms, rs = self.stat[:, 0:nblk], self.stat[:, 4:4 + nblk]
        self.DVE.wait(summed)
        mean = self.ts(ms, self.bank[bs][:, 0:nblk], 1.0 / D, ALU.mult, s2=EPS, op1=ALU.add)
        self.bank_read[bs] = [mean]
        self.POOL.wait(mean)
        root = self.tt(rs, ms, self.c("half_neg", 0, nblk), ALU.pow, engine=self.POOL)
        self.PE.wait(root, self.bank_read[bb])
        for tb in range(nblk):
            rows = self.mm(self.bank[bb][:, tb * P:(tb + 1) * P], rs[:, tb:tb + 1].to_broadcast([P, P]), self.c("ident"),
                           tb == 0, True, skip=True)
        return rows

    def norm_to_h(self, bs, bb, summed, gain, src=None, hi=None, lo=None, width=T, nblk=TB):
        src = src or self.x
        hi, lo = hi or self.hhi, lo or self.hlo
        rows = self.rstd_rows(bs, bb, summed, nblk=nblk)
        parts, scaled = [], []
        for k in range(KT + 1):
            if k < KT:
                t, o = self.tmp[k % 4], slice(k * width, (k + 1) * width)
                self.DVE.wait(rows if k == 0 else None, parts[k - 4] if k >= 4 else None)
                scaled.append(self.stt(t[:, 0:width], src[:, o], gain(k), self.bank[bb][:, 0:width], ALU.mult, ALU.mult))
            if k > 0:
                t, o = self.tmp[(k - 1) % 4], slice((k - 1) * width, k * width)
                self.ACT.wait(scaled[k - 1])
                parts.append(self.split(t[:, 0:width], hi[:, o], lo[:, o]))
        self.bank_read[bb] = [scaled[-1]]
        return parts

    def feed_forward(self, h_parts, post):
        self.names += 1
        put = self.arena(self.at_big, self.big_end)
        ahi, alo = put(f"ff{self.names}_ahi", FT * T, F32R), put(f"ff{self.names}_alo", FT * T, F32R)
        tmp, g = self.tmp, self.g
        with g.loop(FPAIR) as pair:
            for b in range(4):
                self.bank_read[b] = [pair.before(f"bank{b}")]
            sig, gated = [None, None], [None, None]

            def gate(m, b, tile_done):
                self.ACT.wait(tile_done, pair.before(f"split{m}"))
                sig[m] = self.act(tmp[m][:, :], self.bank[b][:, :], ACT.Tanh, scale=0.5)
                self.DVE.wait(sig[m])
                gated[m] = self.stt(tmp[2 + m][:, :], tmp[m][:, :], 1.0, self.bank[b][:, :], ALU.add, ALU.mult)
                pair.names[f"bank{b}"] = gated[m]

            def up(m, b, tile_done):
                self.DVE.wait(tile_done, gated[m])
                a = self.stt(tmp[m][:, :], tmp[2 + m][:, :], 0.5, self.bank[b][:, :], ALU.mult, ALU.mult)
                pair.names[f"bank{b}"] = a
                at = lambda t: (lambda: t[:, bass.ds(pair.var * (2 * T) + m * T, T)])
                self.ACT.wait(a)
                pair.names[f"split{m}"] = self.split(tmp[m][:, :], at(ahi), at(alo))[1]

            self.weights_stationary([0, 1], [self.hhi, self.hlo], KT, gate, ready_k=h_parts)
            self.weights_stationary([2, 3], [self.hhi, self.hlo], KT, up)
        self.bank_read = [[pair.names[f"bank{b}"]] for b in range(4)] + [[] for _ in range(4)]
        self.PE.wait(pair.names["split1"])
        self.ACT.wait(self.PE.latest)
        self.seed_sums(0)
        with g.loop(2) as half:
            for b in range(4, 8):
                self.bank_read[b] = [half.before(f"bank{b}")]
            for two in range(2):
                def evac(m, b, tile_done, two=two):
                    j = two * 2 + m
                    at = lambda t: (lambda: t[:, bass.ds(half.var * (4 * T) + j * T, T)])
                    half.names[f"bank{b}"] = post(at, j, b, tile_done, half)
                for k0, nk in ((0, 8), (8, 8), (16, 6)):
                    self.weights_stationary([4 + 2 * two, 5 + 2 * two], [ahi, alo], nk, evac, k0=k0, ktot=FT)
            self.add_sums_due()
        for b in range(4, 8):
            self.bank_read[b] = [half.names[f"bank{b}"]]
        return half.names["sum3"]

    def ff_residual(self, at, j, b, tile_done, half):
        xs, t = at(self.x), self.tmp[j % 2]
        self.DVE.wait(tile_done)
        added = self.tt(xs, self.bank[b][:, :], xs, ALU.add)
        self.ACT.wait(added, half.before(f"sum{j + 2}") if j < 2 else half.names[f"sum{j - 2}"])
        squared = self.act(t[:, :], xs, ACT.Square)
        self.sum_later(t, 0, squared, lambda count: half.names.__setitem__(f"sum{j}", count))
        return added

    def ff_keep(self, at, j, b, tile_done, half):
        t = self.tmp[j % 2]
        self.ACT.wait(tile_done)
        self.act(at(self.y), self.bank[b][:, :], ACT.Copy)
        self.ACT.wait(half.before(f"sum{j + 2}") if j < 2 else half.names[f"sum{j - 2}"])
        squared = self.act(t[:, :], self.bank[b][:, :], ACT.Square)
        self.sum_later(t, 0, squared, lambda count: half.names.__setitem__(f"sum{j}", count))
        return squared

    def post_norm(self, gain, factor, y, summed):
        rows = self.rstd_rows(0, 1, summed)
        added, scaled = [], []
        self.DVE.wait(rows)
        for k in range(KT + 1):
            if k < KT:
                ys = y[:, k * T:(k + 1) * T]
                scaled.append(self.stt(ys, ys, gain(k), self.bank[1][:, :], ALU.mult, ALU.mult))
            if k > 0:
                before = slice((k - 1) * T, k * T)
                self.DVE.wait(scaled[k - 1])
                added.append(self.stt(self.x[:, before], y[:, before], factor, self.x[:, before], ALU.mult, ALU.add))
        self.bank_read[1] = [scaled[-1]]
        return self.squares_of_x(added)

    def attend(self, units, put, others=iter(()), per_unit=0):
        self.names += 1
        prob = [put(f"att{self.names}_s{i}", T) for i in range(3)]
        probT = [put(f"att{self.names}_p{i}", T) for i in range(2)]
        N = len(units)
        trans_done, pv_done, out_done = {}, {}, {}
        exp_done, trans_kept, weight_done = {}, {}, {}
        for step in range(N + 2):
            if step < N:
                u = units[step]
                n, b, s = u["n"], step % 2, prob[step % 3]
                bias_made = u["make_bias"]() if "make_bias" in u else None
                self.PE.wait(self.bank_read[b])
                scores = self.mm(self.bank[b][:, 0:n], u["q"], u["k"], True, True)
                self.DVE.wait(scores, trans_done.get(step - 3), bias_made)
                if "bias" in u:
                    biased = self.tt(s[:, 0:n], self.bank[b][:, 0:n], u["bias"], ALU.add)
                else:
                    biased = self.stt(s[:, 0:n], u["dist"], u["slope"], self.bank[b][:, 0:n], ALU.mult, ALU.add)
                self.bank_read[b] = [biased]
                st = 32 + 4 * (step % 6)
                neg_max, total, weight = (self.stat[:, st + i:st + i + 1] for i in range(3))
                self.DVE.wait(biased)
                maxed = self.reduce(neg_max, s[:, 0:n], ALU.max, negate=True)
                self.ACT.wait(maxed, out_done.get(step - 6))
                exp_done[step] = self.act(s[:, 0:n], s[:, 0:n], ACT.Exp, bias=neg_max, accum_out=total)
            if 1 <= step < N + 1:
                i = step - 1
                u, n, b, s, p = units[i], units[i]["n"], 2 + i % 2, prob[i % 3], probT[i % 2]
                nb, rows = (n + P - 1) // P, min(n, P)
                self.PE.wait(exp_done[i], self.bank_read[b])
                for kb in range(nb):
                    out, part = self.bank[b][0:rows, kb * P:(kb + 1) * P], s[:, kb * P:kb * P + rows]
                    trans_done[i] = self.PE.do(lambda out=out, part=part: self.nc.tensor.transpose(out, part, self.c("ident")),
                                               signal=kb == nb - 1)
                self.ACT.wait(trans_done[i], pv_done.get(i - 2))
                trans_kept[i] = self.act(p[0:rows, 0:nb * P], self.bank[b][0:rows, 0:nb * P], ACT.Copy)
                self.bank_read[b] = [trans_kept[i]]
                st = 32 + 4 * (i % 6)
                total, weight = self.stat[:, st + 1:st + 2], self.stat[:, st + 2:st + 3]
                self.DVE.wait(exp_done[i])
                floored = self.ts(weight, total, 1e-30, ALU.max)
                self.DVE.wait(floored)
                weight_done[i] = self.reciprocal(weight, weight)
                if "gate" in u:
                    self.DVE.wait(weight_done[i])
                    weight_done[i] = self.ts(weight, weight, u["gate"], ALU.mult)
            if 2 <= step:
                i = step - 2
                u, n, b, p = units[i], units[i]["n"], 4 + i % 2, probT[i % 2]
                nb, rows = (n + P - 1) // P, min(n, P)
                st = 32 + 4 * (i % 6)
                weight = self.stat[:, st + 2:st + 3]
                self.PE.wait(trans_kept[i], self.bank_read[b])
                for kb in range(nb):
                    pv_done[i] = self.mm(self.bank[b][:, 0:DH], p[0:rows, kb * P:(kb + 1) * P], u["v"](kb), kb == 0, kb == nb - 1)
                self.DVE.wait(pv_done[i], weight_done[i])
                if u.get("add"):
                    self.DVE.wait(u["o_before"]())
                    out_done[i] = self.stt(u["o"], self.bank[b][:, 0:DH], weight, u["o"], ALU.mult, ALU.add)
                else:
                    out_done[i] = self.ts(u["o"], self.bank[b][:, 0:DH], weight, ALU.mult)
                self.bank_read[b] = [out_done[i]]
                if "done" in u:
                    u["done"](out_done[i])
            for _ in range(per_unit):
                next(others, None)
        for _ in others:
            pass

    def sigmoid_half(self, out, in_, **kw):
        return self.act(out, in_, ACT.Tanh, scale=0.5, **kw)

    def softplus(self, x, u, w, d, one):
        neg = self.ts(u, x, -1.0, ALU.mult)
        self.DVE.wait(neg)
        neg = self.tt(u, u, x, ALU.min)
        self.ACT.wait(neg)
        exp = self.act(u, u, ACT.Exp)
        self.DVE.wait(exp)
        plus = self.ts(w, u, 1.0, ALU.add)
        self.DVE.wait(plus)
        less = self.tt(d, w, one, ALU.subtract)
        self.DVE.wait(less)
        less = self.ts(d, d, 1e-30, ALU.add)
        self.ACT.wait(less)
        log = self.act(w, w, ACT.Ln)
        self.DVE.wait(less)
        inverse = self.reciprocal(d, d)
        self.DVE.wait(log)
        log = self.ts(w, w, 1e-30, ALU.add)
        self.DVE.wait(log, inverse)
        ratio = self.tt(w, w, d, ALU.mult)
        self.DVE.wait(ratio)
        log1p = self.tt(w, w, u, ALU.mult)
        self.DVE.wait(log1p)
        return self.stt(x, x, 0.0, w, ALU.max, ALU.add)

    def conv4(self, out, raw, bank, w, b, tile_done, raw_read, out_read):
        self.ACT.wait(tile_done, raw_read, out_read)
        shifted = self.act(raw[:, 3:3 + T], self.bank[bank][:, :], ACT.Copy)
        summed = read = self.act(out, self.bank[bank][:, :], ACT.Identity, scale=w(3), bias=b)
        self.DVE.wait(shifted)
        for k in range(3):
            self.DVE.wait(summed)
            summed = self.stt(out, raw[:, k:k + T], w(k), out, ALU.mult, ALU.add)
        return read, summed

    def out_proj(self, acts, nk, post):
        for pair in range(4):
            banks = [2 + 2 * (pair % 2), 3 + 2 * (pair % 2)]

            def evac(m, b, tile_done, pair=pair):
                return post(pair * 2 + m, b, tile_done)
            for k0 in range(0, nk, 8):
                self.weights_stationary(banks, acts, min(8, nk - k0), evac, k0=k0, ktot=nk)
        self.add_sums_due()

    def proj_keep(self, y, added):
        def post(m, b, tile_done):
            t = self.tmp[m % 2]
            self.ACT.wait(tile_done)
            self.act(y[:, m * T:(m + 1) * T], self.bank[b][:, :], ACT.Copy)
            self.ACT.wait(added[m - 2] if m >= 2 else None)
            squared = self.act(t[:, :], self.bank[b][:, :], ACT.Square)
            self.sum_later(t, 0, squared, added.append)
            return squared
        return post

    def proj_residual(self, added):
        def post(m, b, tile_done):
            xs, t = self.x[:, m * T:(m + 1) * T], self.tmp[m % 2]
            self.DVE.wait(tile_done)
            onto = self.tt(xs, self.bank[b][:, :], xs, ALU.add)
            self.ACT.wait(onto, added[m - 2] if m >= 2 else None)
            squared = self.act(t[:, :], xs, ACT.Square)
            self.sum_later(t, 0, squared, added.append)
            return onto
        return post

    def to_bank(self, dst, scale=1.0):
        def evac(m, b, tile_done):
            self.ACT.wait(tile_done)
            return self.act(dst(m), self.bank[b][:, :], ACT.Copy, scale=scale)
        return evac

    def silu_tokens(self, dst, c, used):
        def evac(tb, b, tile_done):
            t, o = self.tmp[tb % 2], dst[:, tb * 512 + c * 256:tb * 512 + c * 256 + 256]
            self.ACT.wait(tile_done, used[tb % 2])
            sig = self.sigmoid_half(t[:, 0:256], self.bank[b][:, 0:256])
            self.DVE.wait(sig)
            used[tb % 2] = self.stt(o, t[:, 0:256], 1.0, self.bank[b][:, 0:256], ALU.add, ALU.mult)
            self.DVE.wait(used[tb % 2])
            self.ts(o, o, 0.5, ALU.mult)
            return used[tb % 2]
        return evac

    def mixer_one(self, h_parts):
        nc = self.nc
        put = self.arena(self.at_big, self.big_end)
        qT, kT = put("m1_q", 4 * T), put("m1_k", 4 * T)
        lru = put("m1_lru", 4 * T)
        v, z = put("m1_v", TB * 512), put("m1_z", TB * 512)
        xbc = put("m1_xbc", 8 * T)
        lw = put("m1_lw", self.dram["lw"].shape[1])
        dt, acs, dta, eacs, edt, cdec = (put(f"m1_dt{i}", 32) for i in range(6))
        small = put("m1_small", 64)
        mark = put.at[0]
        raw = [put(f"m1_raw{i}", T + 4) for i in range(2)]
        conv, rec, inp, gate1, gate0 = (put(f"m1_l{i}", T) for i in range(5))
        room = put("m1_room", 96)
        h = [self.hhi, self.hlo]

        loaded = self.load(lw[:, :], self.dram["lw"], "lw")
        zeros = [self.memset(r[:, 0:3], 0.0) for r in raw]
        ones = self.memset(small[:, 32:64], 1.0)
        lam, half_bias, neg_a = small[:, 0:4], small[:, 4:12], small[:, 12:20]
        negated = self.ts(lam, self.p1("lru_lambda", 0, 4), -1.0, ALU.mult)
        self.DVE.wait(negated, ones, zeros)
        plus = self.softplus(lam, room[:, 0:4], room[:, 32:36], room[:, 64:68], small[:, 32:36])
        self.DVE.wait(plus)
        self.ts(lam, lam, -4.0, ALU.mult)
        o = PAR1["lru_ba"][0]
        half_done = self.ts(half_bias, self.par1[:, o:o + 8], 0.5, ALU.mult)
        exp_a = self.act(neg_a, self.p1("a_log", 0, 8), ACT.Exp)
        self.DVE.wait(exp_a)
        self.ts(neg_a, neg_a, -1.0, ALU.mult)
        self.ACT.wait(half_done)

        for dst, scale in ((qT, DH ** -0.5), (kT, 1.0)):
            for c in range(2):
                self.weights_stationary([4 * c, 4 * c + 1], h, KT, self.to_bank(
                    lambda m, c=c, dst=dst: dst[:, (2 * c + m) * T:(2 * c + m + 1) * T], scale), ready_k=h_parts)
        for c in range(2):
            def evac(tb, b, tile_done, c=c):
                self.ACT.wait(tile_done)
                return self.act(v[:, tb * 512 + c * 256:tb * 512 + c * 256 + 256], self.bank[b][:, 0:256], ACT.Copy)
            self.weights_moving(h, 0, 256, evac, [2, 3, 6, 7])
        used = [None, None]
        for c in range(2):
            self.weights_moving(h, 0, 256, self.silu_tokens(z, c, used), [2, 3, 6, 7])
        self.PE.wait(loaded, self.bank_read[5])
        for tb in range(TB):
            for k in range(KT):
                for part in h:
                    o = k * T + tb * P
                    dt_done = self.mm(self.bank[5][:, tb * 8:tb * 8 + 8], part[:, o:o + P].bitcast(F32), lw[:, 1024 + k * 8:1032 + k * 8],
                                      tb == 0 and k == 0 and part is h[0], True, skip=True)
        self.DVE.wait(dt_done)
        for tb in range(TB):
            biased = self.tt(dt[:, tb * 8:tb * 8 + 8], self.bank[5][:, tb * 8:tb * 8 + 8], self.p1("dt_bias", 0, 8), ALU.add)
        self.bank_read[5] = [biased]
        self.DVE.wait(biased)
        self.softplus(dt[:, :], room[:, 0:32], room[:, 32:64], room[:, 64:96], small[:, 32:64])

        raw_read, tmp_read = [None, None], [None, None]
        for c in range(4):
            def evac(m, b, tile_done, c=c):
                j = 2 * c + m
                out, t = xbc[:, j * T:(j + 1) * T], self.tmp[2 + m]
                read, conved = self.conv4(out, raw[m], b, lambda k: self.p1("ssd_conv_w", k * 8 + j), self.p1("ssd_conv_b", j),
                                          tile_done, raw_read[m], None)
                raw_read[m] = conved
                self.ACT.wait(conved, tmp_read[m])
                sig = self.sigmoid_half(t[:, :], out)
                self.DVE.wait(sig)
                tmp_read[m] = self.stt(out, t[:, :], 1.0, out, ALU.add, ALU.mult)
                self.DVE.wait(tmp_read[m])
                self.ts(out, out, 0.5, ALU.mult)
                return read
            self.weights_stationary([4 * (c % 2), 4 * (c % 2) + 1], h, KT, evac)

        tile_made, gate_kept = None, {}
        state = dict(made=None)
        for c in range(2):
            def keep_gate(m, b, tile_done):
                self.ACT.wait(tile_done, state["made"])
                gate_kept[m] = self.act([gate0, gate1][m][:, :], self.bank[b][:, :], ACT.Copy)
                return gate_kept[m]
            self.weights_stationary([0, 1], h, KT, keep_gate)

            def recurrence(m, b, tile_done, c=c):
                j, g = 2 * c + m, [gate0, gate1][m]
                t0, t1 = self.tmp[0], self.tmp[1]
                read, conved = self.conv4(conv[:, :], raw[m], b, lambda k: self.p1("lru_conv_w", k * 4 + j),
                                          self.p1("lru_conv_b", j), tile_done, raw_read[m], state["made"])
                raw_read[m] = conved
                self.PE.wait(conved, self.bank_read[6], self.bank_read[7])
                r_done = self.mm(self.bank[6][:, :], lw[:, j * P:(j + 1) * P], conv[:, :], True, True)
                i_done = self.mm(self.bank[7][:, :], lw[:, 512 + j * P:512 + (j + 1) * P], conv[:, :], True, True)
                self.ACT.wait(r_done)
                r_gate = self.sigmoid_half(rec[:, :], self.bank[6][:, :], bias=half_bias[:, j:j + 1])
                self.ACT.wait(i_done)
                i_gate = self.sigmoid_half(inp[:, :], self.bank[7][:, :], bias=half_bias[:, 4 + j:5 + j])
                self.bank_read[6], self.bank_read[7] = [r_gate], [i_gate]
                self.DVE.wait(r_gate)
                log_a = self.ts(rec[:, :], rec[:, :], 1.0, ALU.add, s2=lam[:, j:j + 1], op1=ALU.mult)
                self.ACT.wait(log_a)
                tanh = self.act(t0[:, :], rec[:, :], ACT.Tanh)
                self.ACT.wait(tanh)
                a = self.act(rec[:, :], rec[:, :], ACT.Exp)
                self.DVE.wait(a)
                sq = self.tt(t1[:, :], rec[:, :], rec[:, :], ALU.mult)
                self.DVE.wait(sq)
                sq = self.ts(t1[:, :], t1[:, :], 1.0, ALU.add)
                self.DVE.wait(sq)
                sq = self.stt(t0[:, :], t0[:, :], -1.0, t1[:, :], ALU.mult, ALU.mult)
                self.ACT.wait(sq)
                root = self.act(t0[:, :], t0[:, :], ACT.Sqrt)
                self.DVE.wait(i_gate)
                gated = self.stt(inp[:, :], inp[:, :], 1.0, conv[:, :], ALU.add, ALU.mult)
                self.DVE.wait(gated, root)
                u = self.stt(inp[:, :], inp[:, :], 0.5, t0[:, :], ALU.mult, ALU.mult)
                self.DVE.wait(u, i_done)
                scanned = self.DVE.do(lambda: nc.vector.tensor_tensor_scan(conv[:, :], rec[:, :], inp[:, :], 0.0, ALU.mult, ALU.add))
                self.ACT.wait(gate_kept[m], sq)
                cube = self.act(t1[:, :], g[:, :], ACT.Square)
                self.DVE.wait(cube)
                cube = self.ts(t1[:, :], t1[:, :], 0.044715, ALU.mult, s2=1.0, op1=ALU.add)
                self.DVE.wait(cube)
                cube = self.tt(t1[:, :], t1[:, :], g[:, :], ALU.mult)
                self.ACT.wait(cube)
                tanh = self.act(t1[:, :], t1[:, :], ACT.Tanh, scale=math.sqrt(2.0 / math.pi))
                self.DVE.wait(tanh)
                gelu = self.stt(t1[:, :], t1[:, :], 1.0, g[:, :], ALU.add, ALU.mult)
                self.DVE.wait(gelu, scanned)
                state["made"] = self.stt(lru[:, j * T:(j + 1) * T], t1[:, :], 0.5, conv[:, :], ALU.mult, ALU.mult)
                return read
            self.weights_stationary([4, 5], h, KT, recurrence)
        self.barrier()

        put = self.arena(mark, self.big_end)
        bias = [put(f"m1_bias{i}", T) for i in range(2)]
        o_tok = put("m1_otok", TB * 512)
        units, bias_made = [], {}

        def make_bias(hh):
            if hh not in bias_made:
                bias_made[hh] = self.stt(bias[hh % 2][:, :], self.c("dist"), SLOPES[hh], self.c("lncount"), ALU.mult, ALU.add)
            return bias_made[hh]
        for hh in range(HEADS):
            rows = slice(DH * (hh % 2), DH * (hh % 2) + DH)
            for qb in range(TB):
                n, o = (qb + 1) * P, (hh // 2) * T
                units.append(dict(
                    n=n, q=qT[rows, o + qb * P:o + qb * P + P], k=kT[rows, o:o + n],
                    bias=bias[hh % 2][:, T - n:T], make_bias=(lambda hh=hh: make_bias(hh)),
                    v=(lambda kb, hh=hh: v[:, kb * 512 + hh * DH:kb * 512 + (hh + 1) * DH]),
                    o=o_tok[:, qb * 512 + hh * DH:qb * 512 + (hh + 1) * DH]))
        self.attend(units, put)
        self.barrier()

        over = self.arena(self.at_big, mark)
        xhi, xlo = over("m1_xhi", 4 * T, F32R), over("m1_xlo", 4 * T, F32R)
        for j in range(4):
            o = slice(j * T, (j + 1) * T)
            self.split(lru[:, o], xhi[:, o], xlo[:, o])
        self.token_to_cat(o_tok, 0, None)
        self.barrier()

        put = self.arena(mark, self.big_end)
        xtok, btok = put("m1_xtok", TB * 512), put("m1_btok", TB * 256)
        y, ssm, xw, sqs = put("m1_y", TB * 512), put("m1_ssm", 512), put("m1_xw", 512), put("m1_sq", 256)
        kept = [None, None]
        for c in range(TB):
            for b, dst, n, j0 in ((0, xtok[:, c * 512:(c + 1) * 512], 4, 0), (1, btok[:, c * 256:(c + 1) * 256], 2, 4)):
                self.PE.wait(kept[b])
                for j in range(n):
                    o = (j0 + j) * T + c * P
                    turned = self.transpose(self.bank[b][:, j * P:(j + 1) * P], xbc[:, o:o + P])
                self.ACT.wait(turned)
                kept[b] = self.act(dst, self.bank[b][:, 0:n * P], ACT.Copy)
        for c in range(TB):
            scaled = self.tt(dta[:, c * 8:c * 8 + 8], dt[:, c * 8:c * 8 + 8], neg_a, ALU.mult)
        self.PE.wait(scaled)
        running = self.mm(self.bank[2][:, 0:32], self.c("tri"), dta[:, :], True, True)
        whole = self.mm(self.bank[3][:, 0:32], self.c("allones"), dta[:, :], True, True)
        self.ACT.wait(running)
        self.act(acs[:, :], self.bank[2][:, 0:32], ACT.Copy)
        exp_acs = self.act(eacs[:, :], self.bank[2][:, 0:32], ACT.Exp)
        self.ACT.wait(whole)
        exp_whole = self.act(cdec[:, :], self.bank[3][:, 0:32], ACT.Exp)
        self.DVE.wait(exp_whole)
        left = self.tt(edt[:, :], self.bank[3][:, 0:32], acs[:, :], ALU.subtract)
        self.ACT.wait(left)
        exp_left = self.act(edt[:, :], edt[:, :], ACT.Exp)
        self.DVE.wait(exp_left)
        self.tt(edt[:, :], edt[:, :], dt[:, :], ALU.mult)
        self.PE.wait(kept)
        self.DVE.wait(kept)
        self.bank_read = [list(kept), list(kept), [exp_acs], [left], [], [], [], []]
        skip_d = self.p1("d", 0, 8)
        ssm_made, xw_read, y_done, y_off, squared = None, None, [None, None], None, None
        for c in range(TB):
            for gi in range(2):
                Bf = xbc[:, (4 + gi) * T + c * P:(4 + gi) * T + (c + 1) * P]
                Cf = xbc[:, (6 + gi) * T + c * P:(6 + gi) * T + (c + 1) * P]
                bR, bG, bY, bZ = gi, 2 + gi, 4 + gi, 6
                E, M = self.tmp[gi], self.tmp[2 + gi]
                self.PE.wait(self.bank_read[bR])
                for h4 in range(4):
                    col = c * 8 + gi * 4 + h4
                    r_done = self.mm(self.bank[bR][:, h4 * P:(h4 + 1) * P], dta[:, col:col + 1].to_broadcast([P, P]), self.c("tri"),
                                     True, True, skip=True)
                self.PE.wait(self.bank_read[bG])
                g_done = self.mm(self.bank[bG][:, 0:P], Bf, Cf, True, True)
                self.DVE.wait(r_done, y_done[gi])
                for h4 in range(4):
                    col, o = c * 8 + gi * 4 + h4, slice(h4 * P, (h4 + 1) * P)
                    segments = self.stt(E[:, o], self.bank[bR][:, o], acs[:, col:col + 1], self.c("negtri"), ALU.subtract, ALU.add)
                self.bank_read[bR] = [segments]
                self.ACT.wait(segments)
                decays = self.act(E[:, :], E[:, :], ACT.Exp)
                self.DVE.wait(decays, g_done)
                for h4 in range(4):
                    col, o = c * 8 + gi * 4 + h4, slice(h4 * P, (h4 + 1) * P)
                    weighted = self.stt(M[:, o], E[:, o], dt[:, col:col + 1], self.bank[bG][:, 0:P], ALU.mult, ALU.mult)
                self.bank_read[bG] = [weighted]
                self.PE.wait(weighted, self.bank_read[bY])
                for h4 in range(4):
                    o = c * 512 + (gi * 4 + h4) * DH
                    y_done[gi] = self.mm(self.bank[bY][:, h4 * DH:(h4 + 1) * DH], M[:, h4 * P:(h4 + 1) * P], xtok[:, o:o + DH],
                                         True, True, skip=True)
                if c > 0:
                    self.PE.wait(ssm_made, self.bank_read[bZ])
                    y_off = self.mm(self.bank[bZ][:, gi * 256:(gi + 1) * 256], Cf, ssm[:, gi * 256:(gi + 1) * 256], True, True, skip=True)
                self.DVE.wait(y_done[gi], y_off)
                for h4 in range(4):
                    hh, col = gi * 4 + h4, c * 8 + gi * 4 + h4
                    o = slice(c * 512 + hh * DH, c * 512 + (hh + 1) * DH)
                    inner = whole_y = self.stt(y[:, o], xtok[:, o], skip_d[:, hh:hh + 1], self.bank[bY][:, h4 * DH:(h4 + 1) * DH],
                                               ALU.mult, ALU.add)
                    if c > 0:
                        self.DVE.wait(inner)
                        whole_y = self.stt(y[:, o], self.bank[bZ][:, hh * DH:(hh + 1) * DH], eacs[:, col:col + 1], y[:, o],
                                           ALU.mult, ALU.add)
                self.bank_read[bY] = [inner]
            if c > 0:
                self.bank_read[bZ] = [whole_y]
            yc = y[:, c * 512:(c + 1) * 512]
            self.DVE.wait(whole_y)
            gated = self.tt(yc, yc, z[:, c * 512:(c + 1) * 512], ALU.mult)
            self.ACT.wait(gated)
            for gi in range(2):
                o = c * 512 + gi * 256
                self.ACT.wait(squared)
                squared = self.act(sqs[:, :], y[:, o:o + 256], ACT.Square, accum_out=self.stat[:, c * 2 + gi:c * 2 + gi + 1])
            if c < TB - 1:
                self.DVE.wait(xw_read)
                for hh in range(HEADS):
                    o = c * 512 + hh * DH
                    xw_made = self.ts(xw[:, hh * DH:(hh + 1) * DH], xtok[:, o:o + DH], edt[:, c * 8 + hh:c * 8 + hh + 1], ALU.mult)
                self.PE.wait(xw_made, self.bank_read[7])
                for gi in range(2):
                    o = c * 256 + gi * P
                    xw_read = self.mm(self.bank[7][:, gi * 256:(gi + 1) * 256], btok[:, o:o + P], xw[:, gi * 256:(gi + 1) * 256],
                                      True, True, skip=True)
                self.DVE.wait(xw_read, y_off)
                for hh in range(HEADS):
                    so, new = ssm[:, hh * DH:(hh + 1) * DH], self.bank[7][:, hh * DH:(hh + 1) * DH]
                    if c == 0:
                        ssm_made = self.ts(so, new, 1.0, ALU.mult)
                    else:
                        ssm_made = self.stt(so, so, cdec[:, c * 8 + hh:c * 8 + hh + 1], new, ALU.mult, ALU.add)
                self.bank_read[7] = [ssm_made]
        self.DVE.wait(squared)
        mean = self.ts(self.stat[:, 8:16], self.stat[:, 0:8], 1.0 / 256, ALU.mult, s2=SSD_EPS, op1=ALU.add)
        self.POOL.wait(mean)
        root = self.tt(self.stat[:, 16:24], self.stat[:, 8:16], self.c("half_neg", 0, 8), ALU.pow, engine=self.POOL)
        self.DVE.wait(root)
        for n in range(8):
            o = (n // 2) * 512 + (n % 2) * 256
            self.ts(y[:, o:o + 256], y[:, o:o + 256], self.stat[:, 16 + n:17 + n], ALU.mult)
        self.barrier()
        self.token_to_cat(y, 4, lambda j: self.p1("ssd_norm", j))
        self.barrier()

        def cat(k):
            src = (self.hhi, self.hlo) if k < 8 else (xhi, xlo)
            return [a[:, (k % 8) * T:(k % 8 + 1) * T] for a in src]
        self.seed_sums(0)
        added = []
        self.out_proj(cat, 12, self.proj_residual(added))
        return added[-1]

    def token_to_cat(self, src, k0, gain):
        for j in range(4):
            b, t = j, self.tmp[j]
            for tb in range(TB):
                turned = self.transpose(self.bank[b][:, tb * P:(tb + 1) * P], src[:, tb * 512 + j * P:tb * 512 + (j + 1) * P])
            if gain is None:
                self.ACT.wait(turned)
                kept = self.act(t[:, :], self.bank[b][:, :], ACT.Copy)
            else:
                self.DVE.wait(turned)
                kept = self.ts(t[:, :], self.bank[b][:, :], gain(j), ALU.mult)
            o = slice((k0 + j) * T, (k0 + j + 1) * T)
            self.ACT.wait(kept)
            self.split(t[:, :], self.hhi[:, o], self.hlo[:, o])

    def mixer_two(self, h_parts):
        put = self.arena(self.at_big, self.big_end)
        qT, qr, kr = put("m2_q", 4 * T), put("m2_qr", 4 * T), put("m2_kr", 4 * T)
        kdup = [[put(f"m2_k{n}{gi}", T) for gi in range(2)] for n in "sw"]
        vtok = [put(f"m2_v{n}", TB * P) for n in "sw"]
        gates = put("m2_gates", TB * 24)
        vr, gr = put("m2_vr", TB * 512), put("m2_gr", TB * 512)
        kcmp, vcmp = put("m2_kc", DH), put("m2_vc", P)
        self.mem_k, self.mem_v = put("xa_k", 8 * MEM), put("xa_v", 2 * D)
        self.mem_end = mark = put.at[0]
        U = [[put(f"m2_U{kv}{gi}", 264) for gi in range(2)] for kv in range(2)]
        at_qr, NV = self.at_big + 4 * T * 4, 16 * 66 + P - 66
        place = [put, self.arena(at_qr, at_qr + 8 * T * 4)]
        V = [[place[kv](f"m2_V{kv}{n}", NV, dt) for n, dt in enumerate((F32, F32R, F32R))] for kv in range(2)]
        hid, pe_sum = put("m2_hid", 2 * 66), put("m2_pe", 8)
        h = [self.hhi, self.hlo]

        for c in range(2):
            self.weights_stationary([2 + 2 * c, 3 + 2 * c], h, KT, self.to_bank(
                lambda m, c=c: qT[:, (2 * c + m) * T:(2 * c + m + 1) * T], DH ** -0.5), ready_k=h_parts)
        for kv in range(2):
            for gi in range(2):
                self.memset(U[kv][gi][:, 256:264], 0.0)

        def evac_u(m, b, tile_done):
            self.DVE.wait(tile_done)
            for gi in range(2):
                by_parity = self.bank[b][gi * DH:(gi + 1) * DH, :].rearrange("p (t two) -> p two t", two=2)
                for par in range(2):
                    kept = self.copy(U[m][gi][par * DH:(par + 1) * DH, 0:256], by_parity[:, par, :])
            return kept
        self.weights_stationary([0, 1], h, KT, evac_u)
        V_parts = []
        for kv in range(2):
            whole, hi, lo = V[kv]
            V3 = whole[:, 0:16 * 66].rearrange("p (l c) -> p l c", c=66)
            self.DVE.wait(self.DVE.latest)
            for gi in range(2):
                for a8 in range(2):
                    self.copy(V3[:, a8 * 8:(a8 + 1) * 8, gi * 32:(gi + 1) * 32],
                              U[kv][gi][:, a8 * 8:a8 * 8 + 256].rearrange("p (n r) -> p r n", r=8))
            for e in range(2):
                self.copy(V3[:, :, 64 + e], self.p2("cmp_pe", kv * 16, 16))
            placed = self.memset(whole[:, 16 * 66:NV], 0.0)
            self.ACT.wait(placed)
            V_parts.append(self.split(whole[:, :], hi[:, :], lo[:, :]))
        for n in range(2):
            def keys(hi, lo, n=n):
                b = 4 + n
                self.PE.wait(self.bank_read[b])
                for k in range(KT):
                    ws = [w[:, k * 256:k * 256 + P] for w in (hi, lo)]
                    keys_done = self.mm3(self.bank[b][:, :], ws, [a[:, k * T:(k + 1) * T] for a in h], k == 0, k == KT - 1)
                self.ACT.wait(keys_done)
                for gi in range(2):
                    kept = self.act(kdup[n][gi][0:DH, :], self.bank[b][gi * DH:(gi + 1) * DH, :], ACT.Copy)
                self.DVE.wait(kept)
                for gi in range(2):
                    kept = self.copy(kdup[n][gi][DH:P, :], self.bank[b][gi * DH:(gi + 1) * DH, :])
                self.bank_read[b] = [kept]

            def evac(tb, b, tile_done, n=n):
                self.ACT.wait(tile_done)
                return self.act(vtok[n][:, tb * P:(tb + 1) * P], self.bank[b][:, 0:P], ACT.Copy)
            self.weights_moving(h, P, P, evac, [2, 3, 6, 7], also=keys)
        def gates_body(hi, lo):
            t = self.tmp[0]
            self.PE.wait(self.bank_read[0], self.bank_read[1])
            for k in range(KT):
                made = self.mm3(self.bank[0][:, :], [w[:, k * 256:k * 256 + P] for w in (hi, lo)],
                                [a[:, k * T:(k + 1) * T] for a in h], k == 0, k == KT - 1)
                yield
            self.ACT.wait(made)
            tanh = self.sigmoid_half(t[:, :], self.bank[0][:, :])
            self.bank_read[0] = [tanh]
            self.PE.wait(tanh)
            for tb in range(TB):
                turned = self.transpose(self.bank[1][:, tb * P:(tb + 1) * P], t[:, tb * P:(tb + 1) * P])
            self.DVE.wait(turned)
            sig = self.ts(gates[:, :].rearrange("p (t c) -> p t c", c=24),
                          self.bank[1][:, :].rearrange("p (t c) -> p t c", c=P)[:, :, 0:24], 1.0, ALU.add, s2=0.5, op1=ALU.mult)
            self.bank_read[1] = [sig]
            self.DVE.wait(sig)
            for tb in range(TB):
                compressed = gates[:, tb * 24:(tb + 1) * 24].rearrange("p (h b) -> p h b", b=3)[:, :, 0]
                self.ts(compressed, compressed, self.c("rowvalid", tb, 1), ALU.mult)
            return made
        for _ in self.chunk(gates_body):
            pass

        w2k = self.p2("cmp_w2k", 0, 256)
        w2v = self.p2("cmp_w2v", 0, 128)
        for kv in range(2):
            moving = (lambda k, kv=kv: [a[:, k * 66:k * 66 + P] for a in V[kv][1:]])
            hidden = []

            def evac(m, b, tile_done):
                pb, hm, t = pe_sum[:, m:m + 1], hid[:, m * 66:m * 66 + DH], self.tmp[2 + m][:, 0:DH]
                self.ACT.wait(tile_done)
                kept = self.act(pb, self.bank[b][:, 64:65], ACT.Copy)
                self.DVE.wait(kept)
                summed = self.ts(hm, self.bank[b][:, 0:DH], pb, ALU.add)
                self.ACT.wait(summed)
                tanh = self.sigmoid_half(t, hm)
                self.DVE.wait(tanh)
                silu2 = self.stt(hm, t, 1.0, hm, ALU.add, ALU.mult)
                self.DVE.wait(silu2)
                hidden.append(self.ts(hm, hm, 0.5, ALU.mult))
                return summed
            for part in range(2):
                self.weights_stationary([0, 1], moving, 8, evac, k0=part * 8, ktot=16, width=P, ready_k=[V_parts[kv]] * 16)
            self.PE.wait(hidden)
            if kv == 0:
                for m in range(2):
                    made = self.mm(self.bank[2][:, 0:DH], w2k[:, m * P:(m + 1) * P], hid[:, m * 66:m * 66 + DH], m == 0, m == 1)
                self.ACT.wait(made)
                self.bank_read[2] = [self.act(kcmp[:, :], self.bank[2][:, 0:DH], ACT.Copy)]
                hid_read = made
                self.DVE.wait(hid_read)
            else:
                self.PE.wait(self.bank_read[2])
                for gi in range(2):
                    for m in range(2):
                        o = m * 66 + gi * 32
                        made = self.mm(self.bank[2 + gi][0:32, 0:DH], hid[:, o:o + 32], w2v[:, m * DH:(m + 1) * DH], m == 0, m == 1)
                    self.ACT.wait(made)
                    self.act(vcmp[0:32, gi * DH:(gi + 1) * DH], self.bank[2 + gi][0:32, 0:DH], ACT.Copy)
        self.barrier()

        put = self.arena(mark, self.big_end)
        o_tok = put("m2_otok", TB * 512)
        units, so_far = [], {}
        for qb in range(TB):
            for hh in range(HEADS):
                rows, gi, key = slice(DH * (hh % 2), DH * (hh % 2) + DH), hh // 4, (qb, hh)
                o = (hh // 2) * T + qb * P
                for br in range(3):
                    n = 32 if br == 0 else (qb + 1) * P
                    u = dict(n=n, q=qT[rows, o:o + P], slope=SLOPES[hh], gate=gates[:, qb * 24 + hh * 3 + br:qb * 24 + hh * 3 + br + 1],
                             add=br > 0, o=o_tok[:, qb * 512 + hh * DH:qb * 512 + (hh + 1) * DH])
                    if br == 0:
                        u.update(k=kcmp[rows, gi * 32:(gi + 1) * 32], dist=self.c("cmpdist", qb * 32, 32),
                                 v=(lambda kb, gi=gi: vcmp[0:32, gi * DH:(gi + 1) * DH]))
                    else:
                        u.update(k=kdup[br - 1][gi][rows, 0:n], dist=self.c("dist", T - n, n),
                                 v=(lambda kb, gi=gi, br=br: vtok[br - 1][:, kb * P + gi * DH:kb * P + (gi + 1) * DH]))
                    u["o_before"] = (lambda key=key: so_far[key])
                    u["done"] = (lambda o, key=key: so_far.__setitem__(key, o))
                    units.append(u)
        self.attend(units, put, self.others_during_attention(h, qr, kr, vr, gr), 2)
        self.barrier()
        for tb in range(TB):
            squared = self.act(self.tmp[tb][:, :], o_tok[:, tb * 512:(tb + 1) * 512], ACT.Square, accum_out=self.stat[:, tb:tb + 1])
        self.DVE.wait(squared)
        mean = self.ts(self.stat[:, 4:8], self.stat[:, 0:4], 1.0 / 512, ALU.mult, s2=EPS, op1=ALU.add)
        self.POOL.wait(mean)
        root = self.tt(self.stat[:, 8:12], self.stat[:, 4:8], self.c("half_neg", 0, 4), ALU.pow, engine=self.POOL)
        self.DVE.wait(root)
        for tb in range(TB):
            o = o_tok[:, tb * 512:(tb + 1) * 512]
            self.ts(o, o, self.stat[:, 8 + tb:9 + tb], ALU.mult)
        self.barrier()
        self.token_to_cat(o_tok, 0, lambda j: self.p2("nsa_out_g", j))
        self.barrier()
        self.retention(qr, kr, vr, gr, mark)

        put = self.arena(self.at_big, self.big_end)
        self.names += 1
        y = put(f"m2_y{self.names}", KT * T)
        self.seed_sums(0)
        added = []
        self.out_proj([self.hhi, self.hlo], 8, self.proj_keep(y, added))
        return y, added[-1]

    def others_during_attention(self, h, qr, kr, vr, gr):
        for dst, scale in ((qr, 1.0), (kr, 128.0 ** -0.5)):
            for c in range(2):
                yield from self.stationary_steps([6, 7], h, KT, self.to_bank(
                    lambda m, c=c, dst=dst: dst[:, (2 * c + m) * T:(2 * c + m + 1) * T], scale))
        for c in range(2):
            def evac(tb, b, tile_done, c=c):
                self.ACT.wait(tile_done)
                return self.act(vr[:, tb * 512 + c * 256:tb * 512 + c * 256 + 256], self.bank[b][:, 0:256], ACT.Copy)
            yield from self.moving_steps(h, 0, 256, evac, [6, 7])
        used = [None, None]
        for c in range(2):
            yield from self.moving_steps(h, 0, 256, self.silu_tokens(gr, c, used), [6, 7])
        h_read = self.PE.latest

        mhi, mlo, mem = (self.alias_h(f"xa_{n}", i * KT * MEM, KT * MEM, dt) for i, (n, dt) in enumerate(
            (("mhi", F32R), ("mlo", F32R), ("mem", F32))))
        self.ACT.wait(h_read)
        loaded = self.load(mem[:, :], self.dram["mem"], "mem")
        for _ in range(8):
            yield
        self.seed_sums(6)
        added = []
        for k in range(KT):
            t = self.tmp[k % 2]
            self.ACT.wait(loaded if k == 0 else None, added[k - 2] if k >= 2 else used[k])
            squared = self.act(t[:, 0:MEM], mem[:, k * MEM:(k + 1) * MEM], ACT.Square)
            self.PE.wait(squared)
            added.append(self.add_sums(t, 6, nblk=2))
            yield
        parts = self.norm_to_h(6, 7, added[-1], lambda k: self.p2("xa_mem_g", k), mem, mhi, mlo, MEM, 2)
        yield
        for c in range(4):
            def evac(m, b, tile_done, c=c):
                o = (2 * c + m) * MEM
                self.ACT.wait(tile_done)
                return self.act(self.mem_k[:, o:o + MEM], self.bank[b][:, 0:MEM], ACT.Copy)
            yield from self.stationary_steps([6, 7], [mhi, mlo], KT, evac, ready_k=parts, width=MEM)
        for c in range(4):
            def evac(tb, b, tile_done, c=c):
                self.ACT.wait(tile_done)
                return self.act(self.mem_v[:, tb * D + c * 256:tb * D + (c + 1) * 256], self.bank[b][:, 0:256], ACT.Copy)
            yield from self.moving_steps([mhi, mlo], 0, 256, evac, [6, 7], nblk=2, width=MEM)

    def retention(self, qr, kr, vr, gr, mark):
        put = self.arena(mark, self.big_end)
        A = [put(f"m2_A{n}", 512) for n in range(2)]
        kt = [put(f"m2_kt{n}", 512) for n in range(2)]
        state, o = put("m2_state", 512), put("m2_o", TB * 512)
        state_made, inner_done, state_used, cross = None, [None, None], [None, None], None
        heads = [slice(hh * P, (hh + 1) * P) for hh in range(4)]
        for c in range(TB):
            a, ktt, oc = A[c % 2], kt[c % 2], o[:, c * 512:(c + 1) * 512]
            b_scores, b_inner, b_cross, b_turn, b_state = c % 2, 2 + c % 2, 4, 5, 6

            def tok(t, hh, c=c):
                return t[:, hh * T + c * P:hh * T + (c + 1) * P]
            self.PE.wait(self.bank_read[b_scores])
            for hh in range(4):
                scores = self.mm(self.bank[b_scores][:, heads[hh]], tok(kr, hh), tok(qr, hh), True, True, skip=True)
            self.DVE.wait(scores, inner_done[c % 2])
            decayed = self.tt(a[:, :], self.bank[b_scores][:, :], self.c("decay"), ALU.mult)
            self.bank_read[b_scores] = [decayed]
            if c > 0:
                self.PE.wait(self.bank_read[b_cross], state_made)
                for hh in range(4):
                    cross = self.mm(self.bank[b_cross][:, heads[hh]], tok(qr, hh), state[:, heads[hh]], True, True, skip=True)
            if c < TB - 1:
                self.PE.wait(self.bank_read[b_turn])
                for hh in range(4):
                    turned = self.transpose(self.bank[b_turn][:, heads[hh]], tok(kr, hh))
                self.DVE.wait(turned, state_used[c % 2])
                for hh in range(4):
                    kdec = self.ts(ktt[:, heads[hh]], self.bank[b_turn][:, heads[hh]], self.c("kdec", hh, 1), ALU.mult)
                self.bank_read[b_turn] = [kdec]
            vc = [vr[:, c * 512 + hh * P:c * 512 + (hh + 1) * P] for hh in range(4)]
            self.PE.wait(decayed, self.bank_read[b_inner])
            for hh in range(4):
                inner = self.mm(self.bank[b_inner][:, heads[hh]], a[:, heads[hh]], vc[hh], True, True, skip=True)
            inner_done[c % 2] = inner
            self.ACT.wait(inner)
            out = self.act(oc, self.bank[b_inner][:, :], ACT.Copy)
            self.bank_read[b_inner] = [out]
            if c > 0:
                self.DVE.wait(cross, out)
                for hh in range(4):
                    out = self.stt(oc[:, heads[hh]], self.bank[b_cross][:, heads[hh]], self.c("qdec", hh, 1), oc[:, heads[hh]],
                                   ALU.mult, ALU.add)
                self.bank_read[b_cross] = [out]
            if c < TB - 1:
                self.PE.wait(kdec, self.bank_read[b_state])
                for hh in range(4):
                    added = self.mm(self.bank[b_state][:, heads[hh]], ktt[:, heads[hh]], vc[hh], True, True, skip=True)
                state_used[c % 2] = added
                self.DVE.wait(added, cross)
                for hh in range(4):
                    so, new = state[:, heads[hh]], self.bank[b_state][:, heads[hh]]
                    if c == 0:
                        state_made = self.ts(so, new, 1.0, ALU.mult)
                    else:
                        state_made = self.stt(so, so, CHUNK_DEC[hh], new, ALU.mult, ALU.add)
                self.bank_read[b_state] = [state_made]
            total = self.stat[:, c * 4:c * 4 + 4]
            self.DVE.wait(out)
            summed = self.reduce(total, oc.rearrange("p (h e) -> p h e", h=4), ALU.add)
            self.DVE.wait(summed)
            mean = self.ts(total, total, -1.0 / 128, ALU.mult)
            self.DVE.wait(mean)
            for hh in range(4):
                centred = self.ts(oc[:, heads[hh]], oc[:, heads[hh]], self.stat[:, c * 4 + hh:c * 4 + hh + 1], ALU.add)
            self.ACT.wait(centred)
            for hh in range(4):
                squared = self.act(self.tmp[hh][:, 0:P], oc[:, heads[hh]], ACT.Square,
                                   accum_out=self.stat[:, 16 + c * 4 + hh:17 + c * 4 + hh])
        self.DVE.wait(squared)
        var = self.ts(self.stat[:, 32:48], self.stat[:, 16:32], 1.0 / 128, ALU.mult, s2=EPS, op1=ALU.add)
        self.POOL.wait(var)
        root = self.tt(self.stat[:, 48:64], self.stat[:, 32:48], self.c("half_neg", 0, 16), ALU.pow, engine=self.POOL)
        self.DVE.wait(root)
        for c in range(TB):
            for hh in range(4):
                oo = slice(c * 512 + hh * P, c * 512 + (hh + 1) * P)
                self.stt(o[:, oo], o[:, oo], self.stat[:, 48 + c * 4 + hh:49 + c * 4 + hh], gr[:, oo], ALU.mult, ALU.mult)
        self.barrier()
        self.token_to_cat(o, 4, lambda j: self.p2("ret_gn_g", j))
        self.barrier()

    def alias_h(self, name, off, cols, dt=F32):
        return self.nc.alloc_sbuf_tensor_at(name, [P, cols], dt, offset=self.at_h + off * 4)

    def memory_attention(self, h_parts):
        put = self.arena(self.at_big, self.big_end)
        lower = put("xa_q", 8 * T)
        qT, kT, v = lower, self.mem_k, self.mem_v
        put.at[0] = self.mem_end
        s = [put(f"xa_s{n}", MEM) for n in range(2)]
        pt = [put(f"xa_p{n}", 2 * T) for n in range(2)]
        for c in range(4):
            self.weights_stationary([4 * (c % 2), 4 * (c % 2) + 1], [self.hhi, self.hlo], KT, self.to_bank(
                lambda m, c=c: qT[:, (2 * c + m) * T:(2 * c + m + 1) * T], 256.0 ** -0.5), ready_k=h_parts)
        self.barrier()
        kept_split, pv_done, turned = [None, None], [None, None], [None, None]
        for hh in range(4):
            p = pt[hh % 2]
            for qb in range(TB):
                i = hh * TB + qb
                b, bt, ss = i % 2, 2 + i % 2, s[i % 2]
                self.PE.wait(self.bank_read[b])
                for e in range(2):
                    k = 2 * hh + e
                    scores = self.mm(self.bank[b][:, 0:MEM], qT[:, k * T + qb * P:k * T + (qb + 1) * P], kT[:, k * MEM:(k + 1) * MEM],
                                     e == 0, e == 1)
                st = 64 + 4 * (i % 4)
                neg_max, total = self.stat[:, st:st + 1], self.stat[:, st + 1:st + 2]
                self.DVE.wait(scores)
                maxed = self.reduce(neg_max, self.bank[b][:, 0:MEM], ALU.max, negate=True)
                self.ACT.wait(maxed, turned[i % 2])
                exped = self.act(ss[:, :], self.bank[b][:, 0:MEM], ACT.Exp, bias=neg_max, accum_out=total)
                self.bank_read[b] = [exped]
                self.DVE.wait(exped)
                inverse = self.reciprocal(total, total)
                self.DVE.wait(inverse)
                normed = self.ts(ss[:, :], ss[:, :], total, ALU.mult)
                self.PE.wait(normed, self.bank_read[bt])
                for kb in range(2):
                    turned[i % 2] = self.transpose(self.bank[bt][:, kb * P:(kb + 1) * P], ss[:, kb * P:(kb + 1) * P])
                to = p[:, :].rearrange("p (k q) -> p k q", k=2)[:, :, qb * P:(qb + 1) * P]
                self.ACT.wait(turned[i % 2], pv_done[hh % 2])
                kept = self.act(to, self.bank[bt][:, 0:MEM].rearrange("p (k q) -> p k q", k=2), ACT.Copy)
                self.bank_read[bt] = [kept]
            for e in range(2):
                b, t, o = 4 + e, self.tmp[e], slice((2 * hh + e) * T, (2 * hh + e + 1) * T)
                self.PE.wait(kept, self.bank_read[b])
                for kb in range(2):
                    ov = kb * D + hh * 256 + e * P
                    product = self.mm(self.bank[b][:, :], v[:, ov:ov + P], p[:, kb * T:(kb + 1) * T], kb == 0, kb == 1)
                self.ACT.wait(product, kept_split[e])
                out = self.act(t[:, :], self.bank[b][:, :], ACT.Copy)
                self.bank_read[b] = [out]
                self.ACT.wait(out)
                kept_split[e] = self.split(t[:, :], self.hhi[:, o], self.hlo[:, o])[1]
            pv_done[hh % 2] = product
        self.barrier()
        y = self.nc.alloc_sbuf_tensor_at("xa_y", [P, KT * T], F32, offset=self.at_big)
        self.seed_sums(0)
        added = []
        self.out_proj([self.hhi, self.hlo], 8, self.proj_keep(y, added))
        return y, added[-1]

    def build(self):
        nc, g = self.nc, self.g
        x_loaded = []
        for n in range(4):
            if n == 1:
                self.load(self.consts[:, :], self.dram["c"], "const")
                loaded = self.load(self.par1[:, :], self.dram["p1"], "const")
            o = slice(n * 2 * T, (n + 1) * 2 * T)
            x_loaded += [self.load(self.x[:, o], self.dram["x"][:, o], f"x{n}")] * 2
        for e in (self.PE, self.DVE, self.POOL):
            e.wait(loaded)
        summed = self.squares_of_x(x_loaded)
        self.ACT.wait(loaded)
        self.DVE.wait(x_loaded)
        self.split_next_chunk(0, None)
        self.split_next_chunk(1, None)

        h_parts = self.norm_to_h(0, 1, summed, lambda k: self.p1("norm_mix", k))
        summed = self.mixer_one(h_parts)
        self.barrier()
        h_parts = self.norm_to_h(0, 1, summed, lambda k: self.p1("norm_ffn", k))
        summed = self.feed_forward(h_parts, self.ff_residual)
        rows = self.rstd_rows(0, 1, summed)
        self.DVE.wait(rows)
        normed = []
        for k in range(KT):
            xs = self.x[:, k * T:(k + 1) * T]
            normed.append(self.stt(xs, xs, self.p1("norm_final", k), self.bank[1][:, :], ALU.mult, ALU.mult))
        self.bank_read[1] = [normed[-1]]
        summed = self.squares_of_x(normed)
        self.barrier()

        with g.loop(LAYERS) as layer:
            for e in g.engines:
                e.wait([layer.before("end_" + other.name) for other in g.engines])
            loaded = self.load(self.par2[:, :], lambda: self.dram["p2"][bass.ds(layer.var * P, P), :], "par")
            self.DVE.wait(loaded)
            self.y = self.alias_h("ff_y", 0, KT * T)
            h_parts = self.norm_to_h(0, 1, None, lambda k: self.p2("ffn1_pre_g", k))
            summed = self.feed_forward(h_parts, self.ff_keep)
            summed = self.post_norm(lambda k: self.p2("ffn1_post_g", k), 0.5, self.y, summed)
            self.barrier()

            h_parts = self.norm_to_h(0, 1, summed, lambda k: self.p2("mix_pre_g", k))
            y, summed = self.mixer_two(h_parts)
            summed = self.post_norm(lambda k: self.p2("mix_post_g", k), 1.0, y, summed)
            self.barrier()

            h_parts = self.norm_to_h(0, 1, summed, lambda k: self.p2("xa_pre_g", k))
            y, summed = self.memory_attention(h_parts)
            summed = self.post_norm(lambda k: self.p2("xa_post_g", k), 1.0, y, summed)
            self.barrier()

            h_parts = self.norm_to_h(0, 1, summed, lambda k: self.p2("ffn2_pre_g", k))
            summed = self.feed_forward(h_parts, self.ff_keep)
            self.post_norm(lambda k: self.p2("ffn2_post_g", k), 0.5, self.y, summed)
            for e in g.engines:
                layer.names["end_" + e.name] = e.latest
        g.emit()

        w, count = self.dram["w"], self.dram["w"].shape[0]
        raw = [g.sem("raw0"), g.sem("raw1")]
        for s in range(2):
            nc.sync.dma_start(self.raw[s][:, :], w[s]).then_inc(raw[s], 16)
        with nc.sync.Fori(0, count // 2 - 1) as i:
            for s in range(2):
                nc.sync.wait_ge(g.sem("lo"), i * 2 + (s + 1))
                nc.sync.dma_start(self.raw[s][:, :], w[bass.ds(i * 2 + (2 + s), 1), :, :].rearrange("a p c -> (a p) c")).then_inc(raw[s], 16)
        nc.sync.wait_ge(g.sem("dve"), g.final["dve"])
        stored = g.sem("out")
        nc.sync.dma_start(self.dram["out"], self.x[:, :]).then_inc(stored, 16)
        nc.sync.wait_ge(stored, 16)


def build_program(nc, *args):
    k = Kernel(nc, *args)
    k.build()
    return k


def lay_out(i):
    a = {k: np.asarray(v) for k, v in i.items()}
    chunks = []

    def pad(rows):
        c = np.zeros((P, CHUNK), np.float32)
        c[:, :rows.shape[1]] = rows
        chunks.append(c)

    def cols(w, c0, n=256, k0=0, nk=KT):
        s = w[k0 * P:(k0 + nk) * P, c0:c0 + n].reshape(nk, P, n).transpose(1, 0, 2)
        t = np.zeros((P, nk, 256), np.float32)
        t[:, :, :n] = s
        pad(t.reshape(P, nk * 256))

    def ffn(wg, wu, wd):
        for f in range(FPAIR):
            cols(wg, f * 256)
            cols(wu, f * 256)
        for pair in range(4):
            for k0, nk in ((0, 8), (8, 8), (16, 6)):
                cols(wd, pair * 256, 256, k0, nk)

    w = a["w_in"][0]
    for c in range(0, 3072, 256):
        cols(w, c)
    for c in range(2):
        cols(w, 3080 + c * 256)
        cols(w, 3592 + c * 256)
    for pair in range(4):
        cols(a["w_out"][0], pair * 256, 256, 0, 8)
        cols(a["w_out"][0], pair * 256, 256, 8, 4)
    ffn(a["w_gate"][0], a["w_up"][0], a["w_down"][0])
    n1 = len(chunks)
    for l in range(LAYERS):
        ffn(a["ffn1_w_gate_2"][l], a["ffn1_w_up_2"][l], a["ffn1_w_down_2"][l])
        w = a["w_in_2"][l]
        for c in range(0, 1280, 256):
            cols(w, c)
        cols(w, 1280, 24)
        for kv in range(2):
            for part in range(2):
                cols(a["cmp_w1_2"][l, kv], 0, 256, part * 8, 8)
        for c in range(1304, 3352, 256):
            cols(w, c)
        for n in ("xa_wk_2", "xa_wv_2", "w_out_2", "xa_wq_2", "xa_wo_2"):
            for pair in range(4):
                cols(a[n][l], pair * 256)
        ffn(a["ffn2_w_gate_2"][l], a["ffn2_w_up_2"][l], a["ffn2_w_down_2"][l])
    assert n1 % 2 == 0 and len(chunks) % 2 == 0, (n1, len(chunks))
    chunks += [np.zeros((P, CHUNK), np.float32)] * 2

    def vec(v):
        return v.reshape(-1, P).T

    par1 = np.zeros((P, NPAR1), np.float32)
    for name, v in (("norm_mix", vec(a["norm_mix"][0])), ("norm_ffn", vec(a["norm_ffn"][0])),
                    ("ssd_conv_w", np.concatenate([vec(r) for r in a["ssd_conv_w"][0]], 1)),
                    ("ssd_conv_b", vec(a["ssd_conv_b"][0])), ("dt_bias", np.broadcast_to(a["ssd_dt_bias"][0], (P, 8))),
                    ("a_log", np.broadcast_to(a["ssd_a_log"][0], (P, 8))), ("d", np.broadcast_to(a["ssd_d"][0], (P, 8))),
                    ("ssd_norm", vec(a["ssd_norm"][0])), ("lru_conv_w", np.concatenate([vec(r) for r in a["lru_conv_w"][0]], 1)),
                    ("lru_conv_b", vec(a["lru_conv_b"][0])), ("lru_ba", vec(a["lru_ba"][0])), ("lru_bx", vec(a["lru_bx"][0])),
                    ("lru_lambda", vec(a["lru_lambda"][0])), ("norm_final", vec(a["norm_final"]))):
        o, n = PAR1[name]
        par1[:, o:o + n] = v
    lw = np.zeros((P, 1024 + 64), np.float32)
    for n, name in enumerate(("lru_wa", "lru_wx")):
        for b in range(8):
            r = (b % 2) * 64
            lw[r:r + 64, n * 512 + (b // 2) * P + r:n * 512 + (b // 2) * P + r + 64] = a[name][0, b]
    lw[:, 1024:] = a["w_in"][0][:, 3072:3080].reshape(KT, P, 8).transpose(1, 0, 2).reshape(P, 64)
    par2 = np.zeros((LAYERS * P, NPAR2), np.float32)
    for l in range(LAYERS):
        q = par2[l * P:(l + 1) * P]
        for name in ("ffn1_pre_g", "ffn1_post_g", "mix_pre_g", "mix_post_g", "xa_pre_g", "xa_mem_g", "xa_post_g",
                     "ffn2_pre_g", "ffn2_post_g", "nsa_out_g", "ret_gn_g"):
            o, n = PAR2[name]
            q[:, o:o + n] = vec(a[name + "_2"][l])
        o, n = PAR2["cmp_pe"]
        q[:, o:o + n] = a["cmp_pe_2"][l].reshape(2, 16, P).transpose(2, 0, 1).reshape(P, 32)
        o, n = PAR2["cmp_w2k"]
        wk = a["cmp_w2_2"][l, 0].reshape(2, P, 64).transpose(1, 0, 2)
        q[:, o:o + n] = np.concatenate([wk, wk], 2).reshape(P, 256)
        o, n = PAR2["cmp_w2v"]
        q[:, o:o + n] = a["cmp_w2_2"][l, 1].reshape(2, P, 64).transpose(1, 0, 2).reshape(P, 128)

    def feature_major(x, n):
        return np.ascontiguousarray(x.reshape(n, KT, P).transpose(2, 1, 0).reshape(P, KT * n))
    return dict(wstream=np.stack(chunks), xT=feature_major(a["x"][0], T), memT=feature_major(a["mem_2"][0], MEM),
                consts=CONSTS, par1=par1, lru_w=lw, par2=par2)


def kernel(**inputs):
    import concourse.bacc as bacc
    from concourse.bass_utils import run_bass_kernel_spmd

    nc = bacc.Bacc("TRN2", target_bir_lowering=False, num_devices=1)
    arrays = lay_out(inputs)
    args = [nc.dram_tensor(name, a.shape, mybir.dt.from_np(a.dtype), kind="ExternalInput").ap() for name, a in arrays.items()]
    args.append(nc.dram_tensor("outT", (P, KT * T), F32, kind="ExternalOutput").ap())
    build_program(nc, *args)
    r = run_bass_kernel_spmd(nc, [arrays], core_ids=[0])
    out = r.results[0]["outT"]
    return np.ascontiguousarray(out.reshape(P, KT, T).transpose(2, 1, 0).reshape(1, T, D))
```

```python
import math
from contextlib import contextmanager

import numpy as np
import concourse.bass as bass
from concourse import mybir

F32 = mybir.dt.float32
F32R = mybir.dt.float32r
ACT = mybir.ActivationFunctionType
ALU = mybir.AluOpType
AX_X = mybir.AxisListType.X
ET = mybir.EngineType

P = 128
T = 512
TB = T // P
D = 1024
KT = D // P
MEM = 256
CHUNK = 2048
FF = 2816
FT = FF // P
FPAIR = FT // 2
LAYERS = 2
HEADS = 8
DH = 64
NEG = -1e30
EPS = 1e-6
SSD_EPS = 1e-5
MAIN = (mybir.EngineType.PE, mybir.EngineType.Activation, mybir.EngineType.DVE, mybir.EngineType.Pool)

CONST_COLS = {}


def const_table():
    i = np.arange(P)
    parts = []

    def add(name, a):
        CONST_COLS[name] = (sum(p.shape[1] for p in parts), a.shape[1])
        parts.append(a.astype(np.float32))

    add("ident", np.eye(P))
    add("ones", np.ones((P, 1)))
    add("zeros", np.zeros((P, P)))
    add("half_neg", -0.5 * np.ones((P, 16)))
    d = i[:, None] - (np.arange(T)[None, :] - (T - P))
    add("dist", np.where(d >= 0, -d, NEG))
    count = (d <= 128).astype(int) + (d % 4 == 0) + (d % 16 == 0)
    add("lncount", np.where((d >= 0) & (count > 0), np.log(np.maximum(count, 1)), NEG))
    add("tri", (i[:, None] <= i[None, :]) * 1.0)
    add("allones", np.ones((P, P)))
    add("negtri", np.where(i[None, :] >= i[:, None], 0.0, NEG))
    log_g = [math.log(1.0 - 2.0 ** (-5.0 - h)) for h in range(4)]
    diff = i[None, :] - i[:, None]
    add("decay", np.concatenate([np.where(diff >= 0, np.exp(np.maximum(diff, 0) * g), 0.0) for g in log_g], 1))
    add("qdec", np.stack([np.exp((i + 1.0) * g) for g in log_g], 1))
    add("kdec", np.stack([np.exp((P - 1.0 - i) * g) for g in log_g], 1))
    n = np.arange(32)
    t = (np.arange(TB)[:, None, None] * P + i[None, :, None])
    cm = np.where((n * 16 + 31 <= t) & (n < 31), -(t - (n * 16 + 15.5)), NEG)
    add("cmpdist", cm.transpose(1, 0, 2).reshape(P, -1))
    add("rowvalid", (t[:, :, 0] >= 31).T * 1.0)
    return np.concatenate(parts, 1)


CONSTS = const_table()
CHUNK_DEC = [math.exp(P * math.log(1.0 - 2.0 ** (-5.0 - h))) for h in range(4)]
SLOPES = [2.0 ** -(h + 1) for h in range(HEADS)]

PAR1 = {}
PAR2 = {}


def _cols(table, spec):
    at = 0
    for name, n in spec:
        table[name] = (at, n)
        at += n
    return at


NPAR1 = _cols(PAR1, [("norm_mix", 8), ("norm_ffn", 8), ("ssd_conv_w", 32), ("ssd_conv_b", 8), ("dt_bias", 8),
                     ("a_log", 8), ("d", 8), ("ssd_norm", 4), ("lru_conv_w", 16), ("lru_conv_b", 4),
                     ("lru_ba", 4), ("lru_bx", 4), ("lru_lambda", 4), ("norm_final", 8)])
NPAR2 = _cols(PAR2, [("ffn1_pre_g", 8), ("ffn1_post_g", 8), ("mix_pre_g", 8), ("mix_post_g", 8), ("xa_pre_g", 8),
                     ("xa_mem_g", 8), ("xa_post_g", 8), ("ffn2_pre_g", 8), ("ffn2_post_g", 8), ("nsa_out_g", 4),
                     ("ret_gn_g", 4), ("cmp_pe", 32), ("cmp_w2k", 256), ("cmp_w2v", 128)])


class Count:
    def __init__(self, sem, loops):
        self.sem, self.loops, self.value = sem, loops, None


class Before:
    def __init__(self, loop, name):
        self.loop, self.name = loop, name


class Chunks:
    def __init__(self, sem, mul, off):
        self.sem, self.mul, self.off = sem, mul, off


class Item:
    def __init__(self, engine, what, count, inc, loops):
        self.engine, self.what, self.count, self.inc, self.loops = engine, what, count, inc, loops
        self.chunks = 0


class Loop:
    def __init__(self, n):
        self.n, self.items, self.var, self.per, self.names = n, [], None, {}, {}

    def before(self, name):
        return Before(self, name)


class Engine:
    def __init__(self, queue, name, handle):
        self.queue, self.name, self.handle, self.latest = queue, name, handle, None

    def wait(self, *counts):
        for c in counts:
            if isinstance(c, (list, tuple)):
                self.wait(*c)
            elif c is not None:
                self.queue.add(Item(self, c, None, 0, tuple(self.queue.loops)))

    def do(self, fn, signal=True, sem=None, inc=1):
        count = Count(sem or self.name, tuple(self.queue.loops)) if signal else None
        self.queue.add(Item(self, fn, count, inc, tuple(self.queue.loops)))
        if sem is None:
            self.latest = count
        return count


class Queue:
    def __init__(self, nc):
        self.nc, self.items, self.loops, self.sems = nc, [[]], [], {}
        self.PE, self.ACT, self.DVE, self.POOL = (Engine(self, n, e) for n, e in (
            ("pe", nc.tensor), ("act", nc.scalar), ("dve", nc.vector), ("pool", nc.gpsimd)))
        self.engines = (self.PE, self.ACT, self.DVE, self.POOL)

    def add(self, item):
        self.items[-1].append(item)

    def sem(self, name):
        if name not in self.sems:
            self.sems[name] = self.nc.alloc_semaphore("s_" + name)
        return self.sems[name]

    @contextmanager
    def loop(self, n):
        l = Loop(n)
        self.add(l)
        self.items.append(l.items)
        self.loops.append(l)
        yield l
        self.items.pop()
        self.loops.pop()

    def barrier(self):
        reached = [e.latest for e in self.engines if e.latest is not None]
        for e in self.engines:
            e.wait(*reached)

    def number(self, items, at):
        for it in items:
            if isinstance(it, Loop):
                before = dict(at)
                self.number(it.items, at)
                for sem in at:
                    it.per[sem] = at[sem] - before.get(sem, 0)
                    at[sem] += (it.n - 1) * it.per[sem]
            elif it.count is not None:
                at[it.count.sem] = at.get(it.count.sem, 0) + it.inc
                it.count.value = at[it.count.sem]
            else:
                it.chunks = at.get("hi", 0)

    def value(self, wait):
        c, factors = wait.what, {}
        if isinstance(c, Chunks):
            return c.sem, wait.chunks * c.mul + c.off, {l: l.per.get("hi", 0) * c.mul for l in wait.loops}
        back = None
        if isinstance(c, Before):
            back, c = c.loop, c.loop.names[c.name]
        value = c.value
        for l in c.loops:
            per = l.per[c.sem]
            if l is back:
                value -= per
            if l in wait.loops:
                factors[l] = per
            else:
                value += (l.n - 1) * per
        assert value > 0, "a wait's value has to be positive in the first iteration too"
        return c.sem, value, factors

    def emit(self):
        self.final = {}
        self.number(self.items[0], self.final)
        self.emit_items(self.items[0])

    def emit_items(self, items):
        for it in items:
            if isinstance(it, Loop):
                with self.nc.Fori(0, it.n, engines=MAIN) as it.var:
                    self.emit_items(it.items)
            elif callable(it.what):
                ins = it.what()
                if it.count is not None:
                    ins.then_inc(self.sem(it.count.sem), it.inc)
            else:
                sem, value, factors = self.value(it)
                for l, per in factors.items():
                    if per:
                        value = l.var * per + value
                it.engine.handle.wait_ge(self.sem(sem), value)


def spread(columns, n):
    return columns.rearrange("p (t o) -> p t o", o=1).to_broadcast([P, n, DH])


class Kernel:
    def __init__(self, nc, wstream, xT, memT, consts, par1, lru_w, par2, outT):
        self.nc = nc
        self.g = Queue(nc)
        self.PE, self.ACT, self.DVE, self.POOL = self.g.engines
        self.dram = dict(w=wstream, x=xT, mem=memT, c=consts, p1=par1, lw=lru_w, p2=par2, out=outT)
        self.names = 0
        self.slot = 0
        self.norm_follows = False
        self.sums_due = []
        self.place_memory()

    def place_memory(self):
        nc = self.nc
        self.top = (nc.sbuf_base + 63) // 64 * 64

        def put(name, cols, dt=F32, at=None):
            t = nc.alloc_sbuf_tensor_at(name, [P, cols], dt, offset=self.top if at is None else at)
            if at is None:
                self.top += (cols * 4 + 63) // 64 * 64
            return t

        self.put = put
        self.raw = [put(f"raw{s}", CHUNK) for s in range(2)]
        self.whi = [put(f"whi{s}", CHUNK, F32R) for s in range(2)]
        self.wlo = [put(f"wlo{s}", CHUNK, F32R) for s in range(2)]
        self.x = put("x", KT * T)
        self.at_h = self.top
        self.hhi = put("hhi", KT * T, F32R)
        self.hlo = put("hlo", KT * T, F32R)
        self.consts = put("consts", CONSTS.shape[1])
        self.par1 = put("par1", NPAR1)
        self.par2 = put("par2", NPAR2)
        self.tmp = [put(f"tmp{n}", T) for n in range(4)]
        self.stat = put("stat", 160)
        self.at_big = self.top
        self.big_end = nc.sbuf_usable_end
        self.bank = [nc.alloc_psum_tensor(f"bank{b}", [P, T], F32) for b in range(8)]
        self.bank_read = [[] for _ in range(8)]

    def arena(self, start, end):
        at = [start]

        def put(name, cols, dt=F32):
            t = self.nc.alloc_sbuf_tensor_at(name, [P, cols], dt, offset=at[0])
            at[0] += (cols * 4 + 31) // 32 * 32
            assert at[0] <= end, (name, at[0] - end)
            return t
        put.at = at
        return put

    def c(self, name, a=0, n=None):
        o, w = CONST_COLS[name]
        return self.consts[:, o + a:o + (w if n is None else a + n)]

    def p1(self, name, a=0, n=1):
        o = PAR1[name][0]
        return self.par1[:, o + a:o + a + n]

    def p2(self, name, a=0, n=1):
        o = PAR2[name][0]
        return self.par2[:, o + a:o + a + n]

    def r(self, a):
        return a() if callable(a) else a

    def act(self, out, in_, func, **kw):
        return self.ACT.do(lambda: self.nc.scalar.activation(self.r(out), self.r(in_), func, **kw))

    def tt(self, out, a, b, op, engine=None):
        e = engine or self.DVE
        return e.do(lambda: e.handle.tensor_tensor(self.r(out), self.r(a), self.r(b), op))

    def ts(self, out, a, s1, op0, s2=None, op1=None):
        if op1 is None:
            return self.DVE.do(lambda: self.nc.vector.tensor_scalar(self.r(out), self.r(a), s1, None, op0))
        return self.DVE.do(lambda: self.nc.vector.tensor_scalar(self.r(out), self.r(a), s1, s2, op0, op1))

    def stt(self, out, a, s, b, op0, op1):
        return self.DVE.do(lambda: self.nc.vector.scalar_tensor_tensor(self.r(out), self.r(a), s, self.r(b), op0, op1))

    def copy(self, out, a):
        return self.DVE.do(lambda: self.nc.vector.tensor_copy(out, a))

    def memset(self, out, value):
        return self.DVE.do(lambda: self.nc.vector.memset(out, value))

    def reciprocal(self, out, a):
        return self.DVE.do(lambda: self.nc.vector.reciprocal(out, a))

    def reduce(self, out, a, op, negate=None):
        return self.DVE.do(lambda: self.nc.vector.tensor_reduce(out, a, AX_X, op, negate=negate))

    def mm(self, out, lhsT, rhs, start, stop, skip=False):
        return self.PE.do(lambda: self.nc.tensor.matmul(out, lhsT, rhs, start=start, stop=stop, skip_group_check=skip),
                          signal=stop)

    def transpose(self, out, in_):
        n = in_.shape[0]
        return self.PE.do(lambda: self.nc.tensor.transpose(out, in_, self.c("ident")[0:n, 0:n]))

    def load(self, out, in_, sem):
        return self.ACT.do(lambda: self.nc.scalar.dma_start(out, self.r(in_)), sem=sem, inc=16)

    def barrier(self):
        self.g.barrier()
        self.bank_read = [[] for _ in range(8)]

    def split(self, src, hi, lo):
        hi_done = self.act(hi, src, ACT.Copy)
        self.DVE.wait(hi_done)
        lo_done = self.tt(lo, src, lambda: self.r(hi).bitcast(F32), ALU.subtract)
        return [hi_done, lo_done]

    def split_next_chunk(self, slot, products):
        raw, hi, lo = self.raw[slot], self.whi[slot], self.wlo[slot]
        loaded = Chunks(f"raw{slot}", 8, 16 if slot == 0 else 8)
        self.ACT.wait(loaded, products)
        self.ACT.do(lambda: self.nc.scalar.activation(hi[:, :], raw[:, :], ACT.Copy), sem="hi")
        hi_there = Chunks("hi", 1, 0)
        e = self.DVE if self.norm_follows else self.POOL
        e.wait(hi_there, Chunks("lo", 1, -1))
        e.do(lambda: e.handle.tensor_tensor(lo[:, :], raw[:, :], hi[:, :].bitcast(F32), ALU.subtract), sem="lo")

    def chunk(self, body):
        slot = self.slot
        self.PE.wait(Chunks("hi", 1, -1), Chunks("lo", 1, -1))
        products = yield from body(self.whi[slot], self.wlo[slot])
        self.slot ^= 1
        self.split_next_chunk(slot, products)

    def mm3(self, out, l, r, start, stop, signal=False):
        self.mm(out, l[0], r[0], start, False)
        self.mm(out, l[0], r[1], False, False)
        return self.PE.do(lambda: self.nc.tensor.matmul(out, l[1], r[0], start=False, stop=stop), signal=stop or signal)

    def weights_stationary(self, *args, **kw):
        for _ in self.stationary_steps(*args, **kw):
            pass

    def weights_moving(self, *args, **kw):
        for _ in self.moving_steps(*args, **kw):
            pass

    def stationary_steps(self, banks, acts, nk, evac, k0=0, ktot=None, width=T, ready_k=None):
        ktot = ktot or nk
        part = acts if callable(acts) else (lambda k: [a[:, k * width:(k + 1) * width] for a in acts])

        def body(hi, lo):
            for m in range(2):
                b = banks[m]
                if k0 == 0:
                    self.PE.wait(self.bank_read[b])
                for k in range(nk):
                    ws = [w[:, k * 256 + m * P:k * 256 + m * P + P] for w in (hi, lo)]
                    if ready_k is not None and m == 0:
                        self.PE.wait(ready_k[k0 + k])
                    tile_done = self.mm3(self.bank[b][:, 0:width], ws, part(k0 + k), k0 + k == 0, k0 + k == ktot - 1,
                                         signal=k == nk - 1)
                    if k == 4:
                        self.add_sums_due()
                    if width == T or k % 2:
                        yield
                if k0 + nk == ktot:
                    self.bank_read[b] = [evac(m, b, tile_done)]
            return tile_done
        yield from self.chunk(body)

    def moving_steps(self, acts, c0, n, evac, banks, nblk=TB, width=T, also=None):
        def body(hi, lo):
            if also is not None:
                also(hi, lo)
            for tb in range(nblk):
                b = banks[tb % len(banks)]
                self.PE.wait(self.bank_read[b])
                for k in range(KT):
                    ws = [w[:, k * 256 + c0:k * 256 + c0 + n] for w in (hi, lo)]
                    o = k * width + tb * P
                    tile_done = self.mm3(self.bank[b][:, 0:n], [a[:, o:o + P] for a in acts], ws, k == 0, k == KT - 1)
                    if k % 2:
                        yield
                self.bank_read[b] = [evac(tb, b, tile_done)]
            return tile_done
        yield from self.chunk(body)

    def seed_sums(self, b):
        self.PE.wait(self.bank_read[b])
        z = self.c("zeros")
        self.mm(self.bank[b][:, 0:TB], z[:, 0:P], z[:, 0:TB], True, False, skip=True)

    def add_sums(self, sq, b, nblk=TB):
        for tb in range(nblk):
            o = sq[:, tb * P:(tb + 1) * P]
            added = self.PE.do(lambda tb=tb, o=o: self.nc.tensor.matmul(
                self.bank[b][:, tb:tb + 1], o, self.c("ones"), start=False, stop=True, skip_group_check=True),
                signal=tb == nblk - 1)
        return added

    def sum_later(self, sq, b, squared, note):
        self.sums_due.append((sq, b, squared, note))

    def add_sums_due(self):
        for sq, b, squared, note in self.sums_due:
            self.PE.wait(squared)
            note(self.add_sums(sq, b))
        self.sums_due = []

    def square(self, k, src, reads, before=None):
        j = k % 4
        name, t, acc = ("acc", "add1", "add2", "sum3")[j], [self.tmp[n] for n in (2, 0, 1, 3)][j], self.tmp[2]
        self.ACT.wait(before(name) if before else reads.get(name))
        squared = self.act(t[:, :], src, ACT.Square)
        if j in (1, 2):
            self.POOL.wait(squared, reads["add1"] if j == 2 else None)
            reads[name] = self.tt(acc[:, :], acc[:, :], t[:, :], ALU.add, engine=self.POOL)
        if j == 2:
            self.sum_later(acc, 0, reads[name], lambda count: reads.__setitem__("acc", count))
        if j == 3:
            self.sum_later(t, 0, squared, lambda count: reads.__setitem__("sum3", count))
        return squared

    def squares_of_x(self, made):
        self.seed_sums(0)
        acc, added = self.tmp[2], {}
        for k in range(KT):
            t = acc if k == 0 else self.tmp[(0, 1, 3)[k % 3]]
            self.ACT.wait(made[k], added.get(k - 3))
            squared = self.act(t[:, :], self.x[:, k * T:(k + 1) * T], ACT.Square)
            if k > 0:
                self.POOL.wait(squared, added.get(k - 1))
                added[k] = self.tt(acc[:, :], acc[:, :], t[:, :], ALU.add, engine=self.POOL)
        self.PE.wait(added[KT - 1])
        return self.add_sums(acc, 0)

    def rstd_rows(self, bs, bb, summed, nblk=TB):
        ms, rs = self.stat[:, 0:nblk], self.stat[:, 4:4 + nblk]
        self.DVE.wait(summed)
        mean = self.ts(ms, self.bank[bs][:, 0:nblk], 1.0 / D, ALU.mult, s2=EPS, op1=ALU.add)
        self.bank_read[bs] = [mean]
        self.POOL.wait(mean)
        root = self.tt(rs, ms, self.c("half_neg", 0, nblk), ALU.pow, engine=self.POOL)
        self.PE.wait(root, self.bank_read[bb])
        for tb in range(nblk):
            rows = self.mm(self.bank[bb][:, tb * P:(tb + 1) * P], rs[:, tb:tb + 1].to_broadcast([P, P]), self.c("ident"),
                           tb == 0, True, skip=True)
        return rows

    def norm_to_h(self, bs, bb, summed, gain, src=None, hi=None, lo=None, width=T, nblk=TB):
        src = src or self.x
        hi, lo = hi or self.hhi, lo or self.hlo
        rows = self.rstd_rows(bs, bb, summed, nblk=nblk)
        parts, scaled = [], []
        for k in range(KT + 1):
            if k < KT:
                t, o = self.tmp[k % 4], slice(k * width, (k + 1) * width)
                self.DVE.wait(rows if k == 0 else None, parts[k - 4] if k >= 4 else None)
                scaled.append(self.stt(t[:, 0:width], src[:, o], gain(k), self.bank[bb][:, 0:width], ALU.mult, ALU.mult))
            if k > 0:
                t, o = self.tmp[(k - 1) % 4], slice((k - 1) * width, k * width)
                self.ACT.wait(scaled[k - 1])
                parts.append(self.split(t[:, 0:width], hi[:, o], lo[:, o]))
        self.bank_read[bb] = [scaled[-1]]
        return parts

    def feed_forward(self, h_parts, post):
        self.names += 1
        put = self.arena(self.at_big, self.big_end)
        ahi, alo = put(f"ff{self.names}_ahi", FT * T, F32R), put(f"ff{self.names}_alo", FT * T, F32R)
        tmp, g = self.tmp, self.g
        with g.loop(FPAIR) as pair:
            for b in range(4):
                self.bank_read[b] = [pair.before(f"bank{b}")]
            sig, gated = [None, None], [None, None]

            def gate(m, b, tile_done):
                self.ACT.wait(tile_done, pair.before(f"split{m}"))
                sig[m] = self.act(tmp[m][:, :], self.bank[b][:, :], ACT.Tanh, scale=0.5)
                self.DVE.wait(sig[m])
                gated[m] = self.DVE.do(lambda: self.nc.vector.scalar_tensor_tensor(
                    tmp[2 + m][:, :], tmp[m][:, :], 1.0, self.bank[b][:, :], ALU.add, ALU.mult), sem="gated")
                pair.names[f"bank{b}"] = gated[m]

            def up(m, b, tile_done):
                self.DVE.wait(tile_done, gated[m])
                a = self.stt(tmp[m][:, :], tmp[2 + m][:, :], 0.5, self.bank[b][:, :], ALU.mult, ALU.mult)
                pair.names[f"bank{b}"] = a
                at = lambda t: (lambda: t[:, bass.ds(pair.var * (2 * T) + m * T, T)])
                self.ACT.wait(a)
                pair.names[f"split{m}"] = self.split(tmp[m][:, :], at(ahi), at(alo))[1]

            self.weights_stationary([0, 1], [self.hhi, self.hlo], KT, gate, ready_k=h_parts)
            self.weights_stationary([2, 3], [self.hhi, self.hlo], KT, up)
        self.bank_read = [[pair.names[f"bank{b}"]] for b in range(4)] + [[] for _ in range(4)]
        self.PE.wait(pair.before("split1"))
        last_two = [None] * (FT - 2) + [pair.names["split1"]] * 2
        self.seed_sums(0)
        with g.loop(2) as half:
            for b in range(4, 8):
                self.bank_read[b] = [half.before(f"bank{b}")]
            for two in range(2):
                def evac(m, b, tile_done, two=two):
                    j = two * 2 + m
                    at = lambda t: (lambda: t[:, bass.ds(half.var * (4 * T) + j * T, T)])
                    half.names[f"bank{b}"] = post(at, j, b, tile_done, half)
                for k0, nk in ((0, 8), (8, 8), (16, 6)):
                    self.norm_follows = two == 1 and k0 == 16
                    self.weights_stationary([4 + 2 * two, 5 + 2 * two], [ahi, alo], nk, evac, k0=k0, ktot=FT,
                                            ready_k=last_two)
            self.norm_follows = False
            self.add_sums_due()
        for b in range(4, 8):
            self.bank_read[b] = [half.names[f"bank{b}"]]
        return half.names["sum3"]

    def ff_residual(self, at, j, b, tile_done, half):
        xs = at(self.x)
        self.DVE.wait(tile_done)
        added = self.tt(xs, self.bank[b][:, :], xs, ALU.add)
        self.ACT.wait(added)
        self.square(j, xs, half.names, half.before)
        return added

    def ff_keep(self, at, j, b, tile_done, half):
        self.ACT.wait(tile_done)
        self.act(at(self.y), self.bank[b][:, :], ACT.Copy)
        return self.square(j, self.bank[b][:, :], half.names, half.before)

    def post_norm(self, gain, factor, y, summed):
        rows = self.rstd_rows(0, 1, summed)
        added, scaled = [], []
        self.DVE.wait(rows)
        for k in range(KT + 1):
            if k < KT:
                ys = y[:, k * T:(k + 1) * T]
                scaled.append(self.stt(ys, ys, gain(k), self.bank[1][:, :], ALU.mult, ALU.mult))
            if k > 0:
                before = slice((k - 1) * T, k * T)
                self.DVE.wait(scaled[k - 1])
                added.append(self.stt(self.x[:, before], y[:, before], factor, self.x[:, before], ALU.mult, ALU.add))
        self.bank_read[1] = [scaled[-1]]
        return self.squares_of_x(added)

    def attend(self, units, group, finish, put, others=iter(()), per_unit=0):
        self.names += 1
        prob = [put(f"att{self.names}_s{i}", T) for i in range(3)]
        probT = [put(f"att{self.names}_p{i}", T) for i in range(2)]
        N = len(units)
        trans_done, pv_done, exp_done, trans_kept, weights_made, finished = {}, {}, {}, {}, {}, {}

        def sums(g):
            st = 32 + 8 * (g % 3)
            return self.stat[:, st:st + group], self.stat[:, st + 4:st + 4 + group]
        for step in range(N + 2):
            if step < N:
                u, g = units[step], step // group
                n, b, s = u["n"], step % 2, prob[step % 3]
                bias_made = u["make_bias"]() if "make_bias" in u else None
                self.PE.wait(self.bank_read[b])
                scores = self.mm(self.bank[b][:, 0:n], u["q"], u["k"], True, True)
                self.DVE.wait(scores, trans_done.get(step - 3), bias_made)
                if "bias" in u:
                    biased = self.tt(s[:, 0:n], self.bank[b][:, 0:n], u["bias"], ALU.add)
                else:
                    biased = self.stt(s[:, 0:n], u["dist"], u["slope"], self.bank[b][:, 0:n], ALU.mult, ALU.add)
                self.bank_read[b] = [biased]
                neg_max = self.stat[:, 80 + step % 4:81 + step % 4]
                self.DVE.wait(biased, exp_done.get(step - 4))
                maxed = self.reduce(neg_max, s[:, 0:n], ALU.max, negate=True)
                self.ACT.wait(maxed, weights_made.get(g - 3))
                exp_done[step] = self.act(s[:, 0:n], s[:, 0:n], ACT.Exp, bias=neg_max,
                                          accum_out=sums(g)[0][:, step % group:step % group + 1])
            if 1 <= step < N + 1:
                i = step - 1
                u, n, b, s, p = units[i], units[i]["n"], 2 + i % 2, prob[i % 3], probT[i % 2]
                nb, rows = (n + P - 1) // P, min(n, P)
                self.PE.wait(exp_done[i], self.bank_read[b])
                for kb in range(nb):
                    out, part = self.bank[b][0:rows, kb * P:(kb + 1) * P], s[:, kb * P:kb * P + rows]
                    trans_done[i] = self.PE.do(lambda out=out, part=part: self.nc.tensor.transpose(out, part, self.c("ident")),
                                               signal=kb == nb - 1)
                self.ACT.wait(trans_done[i], pv_done.get(i - 2))
                trans_kept[i] = self.act(p[0:rows, 0:nb * P], self.bank[b][0:rows, 0:nb * P], ACT.Copy)
                self.bank_read[b] = [trans_kept[i]]
                if i % group == group - 1:
                    g = i // group
                    total, inverse = sums(g)
                    self.DVE.wait(exp_done[i], finished.get(g - 3))
                    floored = self.ts(inverse, total, 1e-30, ALU.max)
                    self.DVE.wait(floored)
                    weights_made[g] = self.reciprocal(inverse, inverse)
            if 2 <= step:
                i = step - 2
                u, n, g, p = units[i], units[i]["n"], i // group, probT[i % 2]
                nb, rows, b, at = (n + P - 1) // P, min(n, P), 4 + g % 2, i % group * DH
                self.PE.wait(trans_kept[i], self.bank_read[b] if i % group == 0 else None)
                for kb in range(nb):
                    pv_done[i] = self.mm(self.bank[b][:, at:at + DH], p[0:rows, kb * P:(kb + 1) * P], u["v"](kb), kb == 0, kb == nb - 1,
                                         skip=True)
                if i % group == group - 1:
                    self.DVE.wait(pv_done[i], weights_made[g])
                    read, finished[g] = finish(g, self.bank[b][:, 0:group * DH], sums(g)[1])
                    self.bank_read[b] = [read]
            for _ in range(per_unit):
                next(others, None)
        for _ in others:
            pass

    def sigmoid_half(self, out, in_, **kw):
        return self.act(out, in_, ACT.Tanh, scale=0.5, **kw)

    def softplus(self, x, u, w, d, one):
        neg = self.ts(u, x, -1.0, ALU.mult)
        self.DVE.wait(neg)
        neg = self.tt(u, u, x, ALU.min)
        self.ACT.wait(neg)
        exp = self.act(u, u, ACT.Exp)
        self.DVE.wait(exp)
        plus = self.ts(w, u, 1.0, ALU.add)
        self.DVE.wait(plus)
        less = self.tt(d, w, one, ALU.subtract)
        self.DVE.wait(less)
        less = self.ts(d, d, 1e-30, ALU.add)
        self.ACT.wait(less)
        log = self.act(w, w, ACT.Ln)
        self.DVE.wait(less)
        inverse = self.reciprocal(d, d)
        self.DVE.wait(log)
        log = self.ts(w, w, 1e-30, ALU.add)
        self.DVE.wait(log, inverse)
        ratio = self.tt(w, w, d, ALU.mult)
        self.DVE.wait(ratio)
        log1p = self.tt(w, w, u, ALU.mult)
        self.DVE.wait(log1p)
        return self.stt(x, x, 0.0, w, ALU.max, ALU.add)

    def conv4(self, out, raw, bank, w, b, tile_done, raw_read, out_read):
        self.ACT.wait(tile_done, raw_read, out_read)
        shifted = self.act(raw[:, 3:3 + T], self.bank[bank][:, :], ACT.Copy)
        summed = read = self.act(out, self.bank[bank][:, :], ACT.Identity, scale=w(3), bias=b)
        self.DVE.wait(shifted)
        for k in range(3):
            self.DVE.wait(summed)
            summed = self.stt(out, raw[:, k:k + T], w(k), out, ALU.mult, ALU.add)
        return read, summed

    def out_proj(self, acts, nk, post, ready_k=None):
        for pair in range(4):
            banks = [2 + 2 * (pair % 2), 3 + 2 * (pair % 2)]

            def evac(m, b, tile_done, pair=pair):
                return post(pair * 2 + m, b, tile_done)
            for k0 in range(0, nk, 8):
                self.norm_follows = pair == 3 and k0 + 8 >= nk
                self.weights_stationary(banks, acts, min(8, nk - k0), evac, k0=k0, ktot=nk,
                                        ready_k=ready_k if pair == 0 else None)
        self.norm_follows = False
        self.add_sums_due()

    def proj_keep(self, y, reads):
        def post(m, b, tile_done):
            self.ACT.wait(tile_done)
            self.act(y[:, m * T:(m + 1) * T], self.bank[b][:, :], ACT.Copy)
            return self.square(m, self.bank[b][:, :], reads)
        return post

    def proj_residual(self, reads):
        def post(m, b, tile_done):
            xs = self.x[:, m * T:(m + 1) * T]
            self.DVE.wait(tile_done)
            onto = self.tt(xs, self.bank[b][:, :], xs, ALU.add)
            self.ACT.wait(onto)
            self.square(m, xs, reads)
            return onto
        return post

    def to_bank(self, dst, scale=1.0):
        def evac(m, b, tile_done):
            self.ACT.wait(tile_done)
            return self.act(dst(m), self.bank[b][:, :], ACT.Copy, scale=scale)
        return evac

    def silu_tokens(self, dst, c, used):
        def evac(tb, b, tile_done):
            t, o = self.tmp[tb % 2], dst[:, tb * 512 + c * 256:tb * 512 + c * 256 + 256]
            self.ACT.wait(tile_done, used[tb % 2])
            sig = self.sigmoid_half(t[:, 0:256], self.bank[b][:, 0:256])
            self.DVE.wait(sig)
            used[tb % 2] = self.stt(o, t[:, 0:256], 1.0, self.bank[b][:, 0:256], ALU.add, ALU.mult)
            self.DVE.wait(used[tb % 2])
            self.ts(o, o, 0.5, ALU.mult)
            return used[tb % 2]
        return evac

    def mixer_one(self, h_parts):
        nc = self.nc
        put = self.arena(self.at_big, self.big_end)
        qT, kT = put("m1_q", 4 * T), put("m1_k", 4 * T)
        lru = put("m1_lru", 4 * T)
        v, z = put("m1_v", TB * 512), put("m1_z", TB * 512)
        xbc = put("m1_xbc", 8 * T)
        lw = put("m1_lw", self.dram["lw"].shape[1])
        dt, acs, dta, eacs, edt, cdec = (put(f"m1_dt{i}", 32) for i in range(6))
        small = put("m1_small", 64)
        raw = [put(f"m1_raw{i}", T + 4) for i in range(2)]
        room = put("m1_room", 96)
        mark = put.at[0]
        o_tok = put("m1_otok", TB * 512)
        conv, rec, inp, gate1, gate0 = (put(f"m1_l{i}", T) for i in range(5))
        at_attention = mark + TB * 512 * 4
        h = [self.hhi, self.hlo]

        loaded = self.load(lw[:, :], self.dram["lw"], "lw")
        zeros = [self.memset(r[:, 0:3], 0.0) for r in raw]
        ones = self.memset(small[:, 32:64], 1.0)
        lam, half_bias, neg_a = small[:, 0:4], small[:, 4:12], small[:, 12:20]
        negated = self.ts(lam, self.p1("lru_lambda", 0, 4), -1.0, ALU.mult)
        self.DVE.wait(negated, ones, zeros)
        plus = self.softplus(lam, room[:, 0:4], room[:, 32:36], room[:, 64:68], small[:, 32:36])
        self.DVE.wait(plus)
        self.ts(lam, lam, -4.0, ALU.mult)
        o = PAR1["lru_ba"][0]
        half_done = self.ts(half_bias, self.par1[:, o:o + 8], 0.5, ALU.mult)
        exp_a = self.act(neg_a, self.p1("a_log", 0, 8), ACT.Exp)
        self.DVE.wait(exp_a)
        self.ts(neg_a, neg_a, -1.0, ALU.mult)
        self.ACT.wait(half_done)

        for dst, scale in ((qT, DH ** -0.5), (kT, 1.0)):
            for c in range(2):
                self.weights_stationary([4 * c, 4 * c + 1], h, KT, self.to_bank(
                    lambda m, c=c, dst=dst: dst[:, (2 * c + m) * T:(2 * c + m + 1) * T], scale), ready_k=h_parts)
        for c in range(2):
            def evac(tb, b, tile_done, c=c):
                self.ACT.wait(tile_done)
                return self.act(v[:, tb * 512 + c * 256:tb * 512 + c * 256 + 256], self.bank[b][:, 0:256], ACT.Copy)
            self.weights_moving(h, 0, 256, evac, [2, 3, 6, 7])
        self.PE.wait(loaded, self.bank_read[5])
        for tb in range(TB):
            for k in range(KT):
                for part in h:
                    o = k * T + tb * P
                    dt_done = self.mm(self.bank[5][:, tb * 8:tb * 8 + 8], part[:, o:o + P].bitcast(F32), lw[:, 1024 + k * 8:1032 + k * 8],
                                      tb == 0 and k == 0 and part is h[0], True, skip=True)
        self.DVE.wait(dt_done)
        for tb in range(TB):
            biased = self.tt(dt[:, tb * 8:tb * 8 + 8], self.bank[5][:, tb * 8:tb * 8 + 8], self.p1("dt_bias", 0, 8), ALU.add)
        self.bank_read[5] = [biased]
        self.DVE.wait(biased)
        self.softplus(dt[:, :], room[:, 0:32], room[:, 32:64], room[:, 64:96], small[:, 32:64])

        self.barrier()

        raw_read = [None, None]

        def z_and_xbc():
            used = [None, None]
            for c in range(2):
                yield from self.moving_steps(h, 0, 256, self.silu_tokens(z, c, used), [6, 7])
            tmp_read = [None, None]
            for c in range(4):
                def evac(m, b, tile_done, c=c):
                    j = 2 * c + m
                    out, t = xbc[:, j * T:(j + 1) * T], self.tmp[2 + m]
                    read, conved = self.conv4(out, raw[m], b, lambda k: self.p1("ssd_conv_w", k * 8 + j), self.p1("ssd_conv_b", j),
                                              tile_done, raw_read[m], None)
                    raw_read[m] = conved
                    self.ACT.wait(conved, tmp_read[m])
                    sig = self.sigmoid_half(t[:, :], out)
                    self.DVE.wait(sig)
                    tmp_read[m] = self.stt(out, t[:, :], 1.0, out, ALU.add, ALU.mult)
                    self.DVE.wait(tmp_read[m])
                    self.ts(out, out, 0.5, ALU.mult)
                    return read
                yield from self.stationary_steps([6, 7], h, KT, evac)

        put = self.arena(at_attention, self.big_end)
        bias = [put(f"m1_bias{i}", T) for i in range(2)]
        units, bias_made = [], {}

        def make_bias(hh):
            if hh not in bias_made:
                bias_made[hh] = self.stt(bias[hh % 2][:, :], self.c("dist"), SLOPES[hh], self.c("lncount"), ALU.mult, ALU.add)
            return bias_made[hh]
        for hh in range(HEADS):
            rows = slice(DH * (hh % 2), DH * (hh % 2) + DH)
            for qb in range(TB):
                n, o = (qb + 1) * P, (hh // 2) * T
                units.append(dict(
                    n=n, q=qT[rows, o + qb * P:o + qb * P + P], k=kT[rows, o:o + n],
                    bias=bias[hh % 2][:, T - n:T], make_bias=(lambda hh=hh: make_bias(hh)),
                    v=(lambda kb, hh=hh: v[:, kb * 512 + hh * DH:kb * 512 + (hh + 1) * DH])))

        def finish(hh, outputs, inverse):
            o = o_tok[:, :].rearrange("p (t c) -> p t c", t=TB)[:, :, hh * DH:(hh + 1) * DH]
            done = self.tt(o, outputs.rearrange("p (t d) -> p t d", t=TB), spread(inverse, TB), ALU.mult)
            return done, done
        self.attend(units, TB, finish, put, z_and_xbc(), 3)
        self.barrier()

        gate_kept = {}
        state = dict(made=None)
        for c in range(2):
            def keep_gate(m, b, tile_done):
                self.ACT.wait(tile_done, state["made"])
                gate_kept[m] = self.act([gate0, gate1][m][:, :], self.bank[b][:, :], ACT.Copy)
                return gate_kept[m]
            self.weights_stationary([0, 1], h, KT, keep_gate)

            def recurrence(m, b, tile_done, c=c):
                j, g = 2 * c + m, [gate0, gate1][m]
                t0, t1 = self.tmp[0], self.tmp[1]
                read, conved = self.conv4(conv[:, :], raw[m], b, lambda k: self.p1("lru_conv_w", k * 4 + j),
                                          self.p1("lru_conv_b", j), tile_done, raw_read[m], state["made"])
                raw_read[m] = conved
                self.PE.wait(conved, self.bank_read[6], self.bank_read[7])
                r_done = self.mm(self.bank[6][:, :], lw[:, j * P:(j + 1) * P], conv[:, :], True, True)
                i_done = self.mm(self.bank[7][:, :], lw[:, 512 + j * P:512 + (j + 1) * P], conv[:, :], True, True)
                self.ACT.wait(r_done)
                r_gate = self.sigmoid_half(rec[:, :], self.bank[6][:, :], bias=half_bias[:, j:j + 1])
                self.ACT.wait(i_done)
                i_gate = self.sigmoid_half(inp[:, :], self.bank[7][:, :], bias=half_bias[:, 4 + j:5 + j])
                self.bank_read[6], self.bank_read[7] = [r_gate], [i_gate]
                self.DVE.wait(r_gate)
                log_a = self.ts(rec[:, :], rec[:, :], 1.0, ALU.add, s2=lam[:, j:j + 1], op1=ALU.mult)
                self.ACT.wait(log_a)
                tanh = self.act(t0[:, :], rec[:, :], ACT.Tanh)
                self.ACT.wait(tanh)
                a = self.act(rec[:, :], rec[:, :], ACT.Exp)
                self.DVE.wait(a)
                sq = self.tt(t1[:, :], rec[:, :], rec[:, :], ALU.mult)
                self.DVE.wait(sq)
                sq = self.ts(t1[:, :], t1[:, :], 1.0, ALU.add)
                self.DVE.wait(sq)
                sq = self.stt(t0[:, :], t0[:, :], -1.0, t1[:, :], ALU.mult, ALU.mult)
                self.ACT.wait(sq)
                root = self.act(t0[:, :], t0[:, :], ACT.Sqrt)
                self.DVE.wait(i_gate)
                gated = self.stt(inp[:, :], inp[:, :], 1.0, conv[:, :], ALU.add, ALU.mult)
                self.DVE.wait(gated, root)
                u = self.stt(inp[:, :], inp[:, :], 0.5, t0[:, :], ALU.mult, ALU.mult)
                self.DVE.wait(u, i_done)
                scanned = self.DVE.do(lambda: nc.vector.tensor_tensor_scan(conv[:, :], rec[:, :], inp[:, :], 0.0, ALU.mult, ALU.add))
                self.ACT.wait(gate_kept[m], sq)
                cube = self.act(t1[:, :], g[:, :], ACT.Square)
                self.DVE.wait(cube)
                cube = self.ts(t1[:, :], t1[:, :], 0.044715, ALU.mult, s2=1.0, op1=ALU.add)
                self.DVE.wait(cube)
                cube = self.tt(t1[:, :], t1[:, :], g[:, :], ALU.mult)
                self.ACT.wait(cube)
                tanh = self.act(t1[:, :], t1[:, :], ACT.Tanh, scale=math.sqrt(2.0 / math.pi))
                self.DVE.wait(tanh)
                gelu = self.stt(t1[:, :], t1[:, :], 1.0, g[:, :], ALU.add, ALU.mult)
                self.DVE.wait(gelu, scanned)
                state["made"] = self.stt(lru[:, j * T:(j + 1) * T], t1[:, :], 0.5, conv[:, :], ALU.mult, ALU.mult)
                return read
            self.weights_stationary([4, 5], h, KT, recurrence)
        self.barrier()

        over = self.arena(self.at_big, mark)
        xhi, xlo = over("m1_xhi", 4 * T, F32R), over("m1_xlo", 4 * T, F32R)
        for j in range(4):
            o = slice(j * T, (j + 1) * T)
            self.split(lru[:, o], xhi[:, o], xlo[:, o])
        self.token_to_cat(o_tok, 0, None)
        self.barrier()

        put = self.arena(mark, self.big_end)
        xtok, btok = put("m1_xtok", TB * 512), put("m1_btok", TB * 256)
        y, ssm, xw, sqs = put("m1_y", TB * 512), put("m1_ssm", 512), put("m1_xw", 512), put("m1_sq", 256)
        kept = [None, None]
        for c in range(TB):
            for b, dst, n, j0 in ((0, xtok[:, c * 512:(c + 1) * 512], 4, 0), (1, btok[:, c * 256:(c + 1) * 256], 2, 4)):
                self.PE.wait(kept[b])
                for j in range(n):
                    o = (j0 + j) * T + c * P
                    turned = self.transpose(self.bank[b][:, j * P:(j + 1) * P], xbc[:, o:o + P])
                self.ACT.wait(turned)
                kept[b] = self.act(dst, self.bank[b][:, 0:n * P], ACT.Copy)
        for c in range(TB):
            scaled = self.tt(dta[:, c * 8:c * 8 + 8], dt[:, c * 8:c * 8 + 8], neg_a, ALU.mult)
        self.PE.wait(scaled)
        running = self.mm(self.bank[2][:, 0:32], self.c("tri"), dta[:, :], True, True)
        whole = self.mm(self.bank[3][:, 0:32], self.c("allones"), dta[:, :], True, True)
        self.ACT.wait(running)
        self.act(acs[:, :], self.bank[2][:, 0:32], ACT.Copy)
        exp_acs = self.act(eacs[:, :], self.bank[2][:, 0:32], ACT.Exp)
        self.ACT.wait(whole)
        exp_whole = self.act(cdec[:, :], self.bank[3][:, 0:32], ACT.Exp)
        self.DVE.wait(exp_whole)
        left = self.tt(edt[:, :], self.bank[3][:, 0:32], acs[:, :], ALU.subtract)
        self.ACT.wait(left)
        exp_left = self.act(edt[:, :], edt[:, :], ACT.Exp)
        self.DVE.wait(exp_left)
        self.tt(edt[:, :], edt[:, :], dt[:, :], ALU.mult)
        self.PE.wait(kept)
        self.DVE.wait(kept)
        self.bank_read = [list(kept), list(kept), [exp_acs], [left], [], [], [], []]
        skip_d = self.p1("d", 0, 8)
        ssm_made, xw_read, y_done, y_off, squared = None, None, [None, None], None, None
        def weigh(c, gi):
            Bf = xbc[:, (4 + gi) * T + c * P:(4 + gi) * T + (c + 1) * P]
            Cf = xbc[:, (6 + gi) * T + c * P:(6 + gi) * T + (c + 1) * P]
            bR, bG = gi, 2 + gi
            E, M = self.tmp[gi], self.tmp[2 + gi]
            self.PE.wait(self.bank_read[bR])
            for h4 in range(4):
                col = c * 8 + gi * 4 + h4
                r_done = self.mm(self.bank[bR][:, h4 * P:(h4 + 1) * P], dta[:, col:col + 1].to_broadcast([P, P]), self.c("tri"),
                                 True, True, skip=True)
            self.PE.wait(self.bank_read[bG])
            g_done = self.mm(self.bank[bG][:, 0:P], Bf, Cf, True, True)
            self.DVE.wait(r_done, y_done[gi])
            for h4 in range(4):
                col, o = c * 8 + gi * 4 + h4, slice(h4 * P, (h4 + 1) * P)
                segments = self.stt(E[:, o], self.bank[bR][:, o], acs[:, col:col + 1], self.c("negtri"), ALU.subtract, ALU.add)
            self.bank_read[bR] = [segments]
            self.ACT.wait(segments)
            decays = self.act(E[:, :], E[:, :], ACT.Exp)
            self.DVE.wait(decays, g_done)
            for h4 in range(4):
                col, o = c * 8 + gi * 4 + h4, slice(h4 * P, (h4 + 1) * P)
                weighted = self.stt(M[:, o], E[:, o], dt[:, col:col + 1], self.bank[bG][:, 0:P], ALU.mult, ALU.mult)
            self.bank_read[bG] = [weighted]
            return weighted

        weighted = weigh(0, 0)
        for c in range(TB):
            for gi in range(2):
                M, Cf, bY, bZ = self.tmp[2 + gi], xbc[:, (6 + gi) * T + c * P:(6 + gi) * T + (c + 1) * P], 4 + gi, 6
                this = weighted
                if (c, gi) != (TB - 1, 1):
                    weighted = weigh(c + gi, 1 - gi)
                self.PE.wait(this, self.bank_read[bY])
                for h4 in range(4):
                    o = c * 512 + (gi * 4 + h4) * DH
                    y_done[gi] = self.mm(self.bank[bY][:, h4 * DH:(h4 + 1) * DH], M[:, h4 * P:(h4 + 1) * P], xtok[:, o:o + DH],
                                         True, True, skip=True)
                if c > 0:
                    self.PE.wait(ssm_made, self.bank_read[bZ])
                    y_off = self.mm(self.bank[bZ][:, gi * 256:(gi + 1) * 256], Cf, ssm[:, gi * 256:(gi + 1) * 256], True, True, skip=True)
                self.DVE.wait(y_done[gi], y_off)
                for h4 in range(4):
                    hh, col = gi * 4 + h4, c * 8 + gi * 4 + h4
                    o = slice(c * 512 + hh * DH, c * 512 + (hh + 1) * DH)
                    inner = whole_y = self.stt(y[:, o], xtok[:, o], skip_d[:, hh:hh + 1], self.bank[bY][:, h4 * DH:(h4 + 1) * DH],
                                               ALU.mult, ALU.add)
                    if c > 0:
                        self.DVE.wait(inner)
                        whole_y = self.stt(y[:, o], self.bank[bZ][:, hh * DH:(hh + 1) * DH], eacs[:, col:col + 1], y[:, o],
                                           ALU.mult, ALU.add)
                self.bank_read[bY] = [inner]
                if c > 0:
                    self.bank_read[bZ] = [whole_y]
            yc = y[:, c * 512:(c + 1) * 512]
            self.DVE.wait(whole_y)
            gated = self.tt(yc, yc, z[:, c * 512:(c + 1) * 512], ALU.mult)
            self.ACT.wait(gated)
            for gi in range(2):
                o = c * 512 + gi * 256
                self.ACT.wait(squared)
                squared = self.act(sqs[:, :], y[:, o:o + 256], ACT.Square, accum_out=self.stat[:, c * 2 + gi:c * 2 + gi + 1])
            if c < TB - 1:
                self.DVE.wait(xw_read)
                for hh in range(HEADS):
                    o = c * 512 + hh * DH
                    xw_made = self.ts(xw[:, hh * DH:(hh + 1) * DH], xtok[:, o:o + DH], edt[:, c * 8 + hh:c * 8 + hh + 1], ALU.mult)
                self.PE.wait(xw_made, self.bank_read[7])
                for gi in range(2):
                    o = c * 256 + gi * P
                    xw_read = self.mm(self.bank[7][:, gi * 256:(gi + 1) * 256], btok[:, o:o + P], xw[:, gi * 256:(gi + 1) * 256],
                                      True, True, skip=True)
                self.DVE.wait(xw_read, y_off)
                for hh in range(HEADS):
                    so, new = ssm[:, hh * DH:(hh + 1) * DH], self.bank[7][:, hh * DH:(hh + 1) * DH]
                    if c == 0:
                        ssm_made = self.ts(so, new, 1.0, ALU.mult)
                    else:
                        ssm_made = self.stt(so, so, cdec[:, c * 8 + hh:c * 8 + hh + 1], new, ALU.mult, ALU.add)
                self.bank_read[7] = [ssm_made]
        self.DVE.wait(squared)
        mean = self.ts(self.stat[:, 8:16], self.stat[:, 0:8], 1.0 / 256, ALU.mult, s2=SSD_EPS, op1=ALU.add)
        self.POOL.wait(mean)
        root = self.tt(self.stat[:, 16:24], self.stat[:, 8:16], self.c("half_neg", 0, 8), ALU.pow, engine=self.POOL)
        self.DVE.wait(root)
        for n in range(8):
            o = (n // 2) * 512 + (n % 2) * 256
            self.ts(y[:, o:o + 256], y[:, o:o + 256], self.stat[:, 16 + n:17 + n], ALU.mult)
        self.barrier()
        self.token_to_cat(y, 4, lambda j: self.p1("ssd_norm", j))
        self.barrier()

        def cat(k):
            src = (self.hhi, self.hlo) if k < 8 else (xhi, xlo)
            return [a[:, (k % 8) * T:(k % 8 + 1) * T] for a in src]
        self.seed_sums(0)
        reads = {}
        self.out_proj(cat, 12, self.proj_residual(reads))
        return reads["sum3"]

    def token_to_cat(self, src, k0, gain, before=None):
        parts = []
        for j in range(4):
            b, t = j, self.tmp[j]
            self.PE.wait(self.bank_read[b])
            for tb in range(TB):
                turned = self.transpose(self.bank[b][:, tb * P:(tb + 1) * P], src[:, tb * 512 + j * P:tb * 512 + (j + 1) * P])
            e = self.ACT if gain is None else self.DVE
            e.wait(turned, before[j] if before else None)
            if gain is None:
                kept = self.act(t[:, :], self.bank[b][:, :], ACT.Copy)
            else:
                kept = self.ts(t[:, :], self.bank[b][:, :], gain(j), ALU.mult)
            self.bank_read[b] = [kept]
            o = slice((k0 + j) * T, (k0 + j + 1) * T)
            self.ACT.wait(kept)
            parts.append(self.split(t[:, :], self.hhi[:, o], self.hlo[:, o]))
        return parts

    def mixer_two(self, h_parts):
        put = self.arena(self.at_big, self.big_end)
        qT, qr, kr = put("m2_q", 4 * T), put("m2_qr", 4 * T), put("m2_kr", 4 * T)
        kdup = [[put(f"m2_k{n}{gi}", T) for gi in range(2)] for n in "sw"]
        vtok = [put(f"m2_v{n}", TB * P) for n in "sw"]
        gates = put("m2_gates", TB * 24)
        vr, gr = put("m2_vr", TB * 512), put("m2_gr", TB * 512)
        kcmp, vcmp = put("m2_kc", DH), put("m2_vc", P)
        self.at_mem = put.at[0]
        self.mem_k, self.mem_v = put("xa_k", 8 * MEM), put("xa_v", 2 * D)
        self.mem_end = mark = put.at[0]
        U = [[put(f"m2_U{kv}{gi}", 264) for gi in range(2)] for kv in range(2)]
        at_qr, NV = self.at_big + 4 * T * 4, 16 * 66 + P - 66
        place = [put, self.arena(at_qr, at_qr + 8 * T * 4)]
        V = [[place[kv](f"m2_V{kv}{n}", NV, dt) for n, dt in enumerate((F32, F32R, F32R))] for kv in range(2)]
        hid, pe_sum = put("m2_hid", 2 * 66), put("m2_pe", 8)
        h = [self.hhi, self.hlo]

        for c in range(2):
            self.weights_stationary([2 + 2 * c, 3 + 2 * c], h, KT, self.to_bank(
                lambda m, c=c: qT[:, (2 * c + m) * T:(2 * c + m + 1) * T], DH ** -0.5), ready_k=h_parts)
        for kv in range(2):
            for gi in range(2):
                self.memset(U[kv][gi][:, 256:264], 0.0)

        def evac_u(m, b, tile_done):
            self.DVE.wait(tile_done)
            for gi in range(2):
                by_parity = self.bank[b][gi * DH:(gi + 1) * DH, :].rearrange("p (t two) -> p two t", two=2)
                for par in range(2):
                    kept = self.copy(U[m][gi][par * DH:(par + 1) * DH, 0:256], by_parity[:, par, :])
            return kept
        self.weights_stationary([0, 1], h, KT, evac_u)
        V_parts = []
        for kv in range(2):
            whole, hi, lo = V[kv]
            V3 = whole[:, 0:16 * 66].rearrange("p (l c) -> p l c", c=66)
            self.DVE.wait(self.DVE.latest)
            for gi in range(2):
                for a8 in range(2):
                    self.copy(V3[:, a8 * 8:(a8 + 1) * 8, gi * 32:(gi + 1) * 32],
                              U[kv][gi][:, a8 * 8:a8 * 8 + 256].rearrange("p (n r) -> p r n", r=8))
            for e in range(2):
                self.copy(V3[:, :, 64 + e], self.p2("cmp_pe", kv * 16, 16))
            placed = self.memset(whole[:, 16 * 66:NV], 0.0)
            self.ACT.wait(placed)
            V_parts.append(self.split(whole[:, :], hi[:, :], lo[:, :]))
        for n in range(2):
            def keys(hi, lo, n=n):
                b = 4 + n
                self.PE.wait(self.bank_read[b])
                for k in range(KT):
                    ws = [w[:, k * 256:k * 256 + P] for w in (hi, lo)]
                    keys_done = self.mm3(self.bank[b][:, :], ws, [a[:, k * T:(k + 1) * T] for a in h], k == 0, k == KT - 1)
                self.ACT.wait(keys_done)
                for gi in range(2):
                    kept = self.act(kdup[n][gi][0:DH, :], self.bank[b][gi * DH:(gi + 1) * DH, :], ACT.Copy)
                self.DVE.wait(kept)
                for gi in range(2):
                    kept = self.copy(kdup[n][gi][DH:P, :], self.bank[b][gi * DH:(gi + 1) * DH, :])
                self.bank_read[b] = [kept]

            def evac(tb, b, tile_done, n=n):
                self.ACT.wait(tile_done)
                return self.act(vtok[n][:, tb * P:(tb + 1) * P], self.bank[b][:, 0:P], ACT.Copy)
            self.weights_moving(h, P, P, evac, [2, 3, 6, 7], also=keys)
        def gates_body(hi, lo):
            t = self.tmp[0]
            self.PE.wait(self.bank_read[0], self.bank_read[1])
            for k in range(KT):
                made = self.mm3(self.bank[0][:, :], [w[:, k * 256:k * 256 + P] for w in (hi, lo)],
                                [a[:, k * T:(k + 1) * T] for a in h], k == 0, k == KT - 1)
                yield
            self.ACT.wait(made)
            tanh = self.sigmoid_half(t[:, :], self.bank[0][:, :])
            self.bank_read[0] = [tanh]
            self.PE.wait(tanh)
            for tb in range(TB):
                turned = self.transpose(self.bank[1][:, tb * P:(tb + 1) * P], t[:, tb * P:(tb + 1) * P])
            self.DVE.wait(turned)
            sig = self.ts(gates[:, :].rearrange("p (t c) -> p t c", c=24),
                          self.bank[1][:, :].rearrange("p (t c) -> p t c", c=P)[:, :, 0:24], 1.0, ALU.add, s2=0.5, op1=ALU.mult)
            self.bank_read[1] = [sig]
            self.DVE.wait(sig)
            for tb in range(TB):
                compressed = gates[:, tb * 24:(tb + 1) * 24].rearrange("p (h b) -> p h b", b=3)[:, :, 0]
                self.ts(compressed, compressed, self.c("rowvalid", tb, 1), ALU.mult)
            return made
        for _ in self.chunk(gates_body):
            pass

        w2k = self.p2("cmp_w2k", 0, 256)
        w2v = self.p2("cmp_w2v", 0, 128)
        for kv in range(2):
            moving = (lambda k, kv=kv: [a[:, k * 66:k * 66 + P] for a in V[kv][1:]])
            hidden = []

            def evac(m, b, tile_done):
                pb, hm, t = pe_sum[:, m:m + 1], hid[:, m * 66:m * 66 + DH], self.tmp[2 + m][:, 0:DH]
                self.ACT.wait(tile_done)
                kept = self.act(pb, self.bank[b][:, 64:65], ACT.Copy)
                self.DVE.wait(kept)
                summed = self.ts(hm, self.bank[b][:, 0:DH], pb, ALU.add)
                self.ACT.wait(summed)
                tanh = self.sigmoid_half(t, hm)
                self.DVE.wait(tanh)
                silu2 = self.stt(hm, t, 1.0, hm, ALU.add, ALU.mult)
                self.DVE.wait(silu2)
                hidden.append(self.ts(hm, hm, 0.5, ALU.mult))
                return summed
            for part in range(2):
                self.weights_stationary([0, 1], moving, 8, evac, k0=part * 8, ktot=16, width=P, ready_k=[V_parts[kv]] * 16)
            self.PE.wait(hidden)
            if kv == 0:
                for m in range(2):
                    made = self.mm(self.bank[2][:, 0:DH], w2k[:, m * P:(m + 1) * P], hid[:, m * 66:m * 66 + DH], m == 0, m == 1)
                self.ACT.wait(made)
                self.bank_read[2] = [self.act(kcmp[:, :], self.bank[2][:, 0:DH], ACT.Copy)]
                hid_read = made
                self.DVE.wait(hid_read)
            else:
                self.PE.wait(self.bank_read[2])
                for gi in range(2):
                    for m in range(2):
                        o = m * 66 + gi * 32
                        made = self.mm(self.bank[2 + gi][0:32, 0:DH], hid[:, o:o + 32], w2v[:, m * DH:(m + 1) * DH], m == 0, m == 1)
                    self.ACT.wait(made)
                    self.act(vcmp[0:32, gi * DH:(gi + 1) * DH], self.bank[2 + gi][0:32, 0:DH], ACT.Copy)
        self.barrier()

        put = self.arena(mark, self.big_end)
        at_o = put.at[0]
        o_tok = put("m2_otok", TB * 512)
        scaled = put("m2_scaled", 3 * DH)
        units, summed = [], {}
        for qb in range(TB):
            for hh in range(HEADS):
                rows, gi = slice(DH * (hh % 2), DH * (hh % 2) + DH), hh // 4
                o = (hh // 2) * T + qb * P
                for br in range(3):
                    n = 32 if br == 0 else (qb + 1) * P
                    u = dict(n=n, q=qT[rows, o:o + P], slope=SLOPES[hh])
                    if br == 0:
                        u.update(k=kcmp[rows, gi * 32:(gi + 1) * 32], dist=self.c("cmpdist", qb * 32, 32),
                                 v=(lambda kb, gi=gi: vcmp[0:32, gi * DH:(gi + 1) * DH]))
                    else:
                        u.update(k=kdup[br - 1][gi][rows, 0:n], dist=self.c("dist", T - n, n),
                                 v=(lambda kb, gi=gi, br=br: vtok[br - 1][:, kb * P + gi * DH:kb * P + (gi + 1) * DH]))
                    units.append(u)

        def finish(g, outputs, inverse):
            qb, hh = g // HEADS, g % HEADS
            gated = self.tt(inverse, inverse, gates[:, qb * 24 + hh * 3:qb * 24 + hh * 3 + 3], ALU.mult)
            self.DVE.wait(gated, summed.get(g - 1))
            made = self.tt(scaled[:, :].rearrange("p (b d) -> p b d", b=3), outputs.rearrange("p (b d) -> p b d", b=3),
                           spread(inverse, 3), ALU.mult)
            self.DVE.wait(made)
            summed[g] = self.reduce(o_tok[:, qb * 512 + hh * DH:qb * 512 + (hh + 1) * DH],
                                    scaled[:, :].rearrange("p (b d) -> p d b", b=3), ALU.add)
            return made, summed[g]
        self.attend(units, 3, finish, put, self.others_during_attention(h, qr, kr, vr, gr), 2)
        self.barrier()
        for tb in range(TB):
            squared = self.act(self.tmp[tb][:, :], o_tok[:, tb * 512:(tb + 1) * 512], ACT.Square, accum_out=self.stat[:, 100 + tb:101 + tb])
        self.DVE.wait(squared)
        mean = self.ts(self.stat[:, 104:108], self.stat[:, 100:104], 1.0 / 512, ALU.mult, s2=EPS, op1=ALU.add)
        self.POOL.wait(mean)
        root = self.tt(self.stat[:, 108:112], self.stat[:, 104:108], self.c("half_neg", 0, 4), ALU.pow, engine=self.POOL)

        def scale_attention():
            self.DVE.wait(root)
            for tb in range(TB):
                o = o_tok[:, tb * 512:(tb + 1) * 512]
                done = self.ts(o, o, self.stat[:, 108 + tb:109 + tb], ALU.mult)
            return done
        ret = self.retention(qr, kr, vr, gr, at_o + TB * 512 * 4)
        scaled = scale_attention()
        self.PE.wait(scaled)
        cat_made = self.token_to_cat(o_tok, 0, lambda j: self.p2("nsa_out_g", j))
        self.PE.wait(ret["gated"]())
        cat_made += self.token_to_cat(ret["o"], 4, lambda j: self.p2("ret_gn_g", j), cat_made)

        self.names += 1
        y = self.nc.alloc_sbuf_tensor_at(f"m2_y{self.names}", [P, KT * T], F32, offset=self.at_big)
        self.ACT.wait(cat_made)
        self.seed_sums(0)
        reads = {}
        self.out_proj([self.hhi, self.hlo], 8, self.proj_keep(y, reads), ready_k=cat_made)
        return y, reads["sum3"]

    def others_during_attention(self, h, qr, kr, vr, gr):
        for dst, scale in ((qr, 1.0), (kr, 128.0 ** -0.5)):
            for c in range(2):
                yield from self.stationary_steps([6, 7], h, KT, self.to_bank(
                    lambda m, c=c, dst=dst: dst[:, (2 * c + m) * T:(2 * c + m + 1) * T], scale))
        for c in range(2):
            def evac(tb, b, tile_done, c=c):
                self.ACT.wait(tile_done)
                return self.act(vr[:, tb * 512 + c * 256:tb * 512 + c * 256 + 256], self.bank[b][:, 0:256], ACT.Copy)
            yield from self.moving_steps(h, 0, 256, evac, [6, 7])
        used = [None, None]
        for c in range(2):
            yield from self.moving_steps(h, 0, 256, self.silu_tokens(gr, c, used), [6, 7])
        h_read = self.PE.latest

        mhi, mlo, mem = (self.alias_h(f"xa_{n}", i * KT * MEM, KT * MEM, dt) for i, (n, dt) in enumerate(
            (("mhi", F32R), ("mlo", F32R), ("mem", F32))))
        self.ACT.wait(h_read)
        loaded = self.load(mem[:, :], self.dram["mem"], "mem")
        for _ in range(8):
            yield
        self.seed_sums(6)
        added = []
        for k in range(KT):
            t = self.tmp[k % 2]
            self.ACT.wait(loaded if k == 0 else None, added[k - 2] if k >= 2 else used[k])
            squared = self.act(t[:, 0:MEM], mem[:, k * MEM:(k + 1) * MEM], ACT.Square)
            self.PE.wait(squared)
            added.append(self.add_sums(t, 6, nblk=2))
            yield
        parts = self.norm_to_h(6, 7, added[-1], lambda k: self.p2("xa_mem_g", k), mem, mhi, mlo, MEM, 2)
        yield
        for c in range(4):
            def evac(m, b, tile_done, c=c):
                o = (2 * c + m) * MEM
                self.ACT.wait(tile_done)
                return self.act(self.mem_k[:, o:o + MEM], self.bank[b][:, 0:MEM], ACT.Copy)
            yield from self.stationary_steps([6, 7], [mhi, mlo], KT, evac, ready_k=parts, width=MEM)
        for c in range(4):
            def evac(tb, b, tile_done, c=c):
                self.ACT.wait(tile_done)
                return self.act(self.mem_v[:, tb * D + c * 256:tb * D + (c + 1) * 256], self.bank[b][:, 0:256], ACT.Copy)
            yield from self.moving_steps([mhi, mlo], 0, 256, evac, [6, 7], nblk=2, width=MEM)

    def retention(self, qr, kr, vr, gr, at):
        put = self.arena(at, self.big_end)
        A = [put(f"m2_A{n}", 512) for n in range(2)]
        kt = [put(f"m2_kt{n}", 512) for n in range(2)]
        state = put("m2_state", 512)
        o = self.nc.alloc_sbuf_tensor_at("m2_o", [P, TB * 512], F32, offset=self.at_big)
        state_made, inner_done, state_used, cross = None, [None, None], [None, None], None
        heads = [slice(hh * P, (hh + 1) * P) for hh in range(4)]
        for c in range(TB):
            a, ktt, oc = A[c % 2], kt[c % 2], o[:, c * 512:(c + 1) * 512]
            b_scores, b_inner, b_cross, b_turn, b_state = c % 2, 2 + c % 2, 4, 5, 6

            def tok(t, hh, c=c):
                return t[:, hh * T + c * P:hh * T + (c + 1) * P]
            self.PE.wait(self.bank_read[b_scores])
            for hh in range(4):
                scores = self.mm(self.bank[b_scores][:, heads[hh]], tok(kr, hh), tok(qr, hh), True, True, skip=True)
            self.DVE.wait(scores, inner_done[c % 2])
            decayed = self.tt(a[:, :], self.bank[b_scores][:, :], self.c("decay"), ALU.mult)
            self.bank_read[b_scores] = [decayed]
            if c > 0:
                self.PE.wait(self.bank_read[b_cross], state_made)
                for hh in range(4):
                    cross = self.mm(self.bank[b_cross][:, heads[hh]], tok(qr, hh), state[:, heads[hh]], True, True, skip=True)
            if c < TB - 1:
                self.PE.wait(self.bank_read[b_turn])
                for hh in range(4):
                    turned = self.transpose(self.bank[b_turn][:, heads[hh]], tok(kr, hh))
                self.DVE.wait(turned, state_used[c % 2])
                for hh in range(4):
                    kdec = self.ts(ktt[:, heads[hh]], self.bank[b_turn][:, heads[hh]], self.c("kdec", hh, 1), ALU.mult)
                self.bank_read[b_turn] = [kdec]
            vc = [vr[:, c * 512 + hh * P:c * 512 + (hh + 1) * P] for hh in range(4)]
            self.PE.wait(decayed, self.bank_read[b_inner])
            for hh in range(4):
                inner = self.mm(self.bank[b_inner][:, heads[hh]], a[:, heads[hh]], vc[hh], True, True, skip=True)
            inner_done[c % 2] = inner
            self.ACT.wait(inner)
            out = self.act(oc, self.bank[b_inner][:, :], ACT.Copy)
            self.bank_read[b_inner] = [out]
            if c > 0:
                self.DVE.wait(cross, out)
                for hh in range(4):
                    out = self.stt(oc[:, heads[hh]], self.bank[b_cross][:, heads[hh]], self.c("qdec", hh, 1), oc[:, heads[hh]],
                                   ALU.mult, ALU.add)
                self.bank_read[b_cross] = [out]
            if c < TB - 1:
                self.PE.wait(kdec, self.bank_read[b_state])
                for hh in range(4):
                    added = self.mm(self.bank[b_state][:, heads[hh]], ktt[:, heads[hh]], vc[hh], True, True, skip=True)
                state_used[c % 2] = added
                self.DVE.wait(added, cross)
                for hh in range(4):
                    so, new = state[:, heads[hh]], self.bank[b_state][:, heads[hh]]
                    if c == 0:
                        state_made = self.ts(so, new, 1.0, ALU.mult)
                    else:
                        state_made = self.stt(so, so, CHUNK_DEC[hh], new, ALU.mult, ALU.add)
                self.bank_read[b_state] = [state_made]
            total = self.stat[:, c * 4:c * 4 + 4]
            self.DVE.wait(out)
            summed = self.reduce(total, oc.rearrange("p (h e) -> p h e", h=4), ALU.add)
            self.DVE.wait(summed)
            mean = self.ts(total, total, -1.0 / 128, ALU.mult)
            self.DVE.wait(mean)
            for hh in range(4):
                centred = self.ts(oc[:, heads[hh]], oc[:, heads[hh]], self.stat[:, c * 4 + hh:c * 4 + hh + 1], ALU.add)
            self.ACT.wait(centred)
            for hh in range(4):
                squared = self.act(self.tmp[hh][:, 0:P], oc[:, heads[hh]], ACT.Square,
                                   accum_out=self.stat[:, 16 + c * 4 + hh:17 + c * 4 + hh])
        self.DVE.wait(squared)
        var = self.ts(self.stat[:, 32:48], self.stat[:, 16:32], 1.0 / 128, ALU.mult, s2=EPS, op1=ALU.add)
        self.POOL.wait(var)
        root = self.tt(self.stat[:, 48:64], self.stat[:, 32:48], self.c("half_neg", 0, 16), ALU.pow, engine=self.POOL)

        def gated():
            self.DVE.wait(root)
            for c in range(TB):
                for hh in range(4):
                    oo = slice(c * 512 + hh * P, c * 512 + (hh + 1) * P)
                    done = self.stt(o[:, oo], o[:, oo], self.stat[:, 48 + c * 4 + hh:49 + c * 4 + hh], gr[:, oo], ALU.mult, ALU.mult)
            return done
        return dict(o=o, gated=gated)

    def alias_h(self, name, off, cols, dt=F32):
        return self.nc.alloc_sbuf_tensor_at(name, [P, cols], dt, offset=self.at_h + off * 4)

    def memory_attention(self, h_parts):
        put = self.arena(self.at_big, self.big_end)
        qT, kT, v = put("xa_q", 8 * T), self.mem_k, self.mem_v
        put.at[0] = self.mem_end
        s = [put(f"xa_s{n}", MEM) for n in range(3)]
        pt = [put(f"xa_p{n}", 2 * T) for n in range(2)]
        between = self.arena(self.at_big + 8 * T * 4, self.at_mem)
        chi, clo = between("xa_chi", 8 * T, F32R), between("xa_clo", 8 * T, F32R)
        q_made = {}

        def project(c):
            keep = self.to_bank(lambda m: qT[:, (2 * c + m) * T:(2 * c + m + 1) * T], 256.0 ** -0.5)

            def evac(m, b, tile_done):
                q_made[c] = keep(m, b, tile_done)
                return q_made[c]
            yield from self.stationary_steps([6, 7], [self.hhi, self.hlo], KT, evac, ready_k=h_parts)
        for _ in project(0):
            pass
        normed, turned, kept, pv_done, cat_made = {}, {}, {}, {}, {}
        tmp_read = [None, None]
        others = iter(())
        for step in range(4 * TB + 2):
            i = step
            if i < 4 * TB:
                hh, qb, b, ss = i // TB, i % TB, i % 2, s[i % 3]
                if qb == 0:
                    for _ in others:
                        pass
                    others = project(hh + 1) if hh < 3 else iter(())
                self.PE.wait(self.bank_read[b], q_made[hh])
                for e in range(2):
                    k = 2 * hh + e
                    scores = self.mm(self.bank[b][:, 0:MEM], qT[:, k * T + qb * P:k * T + (qb + 1) * P], kT[:, k * MEM:(k + 1) * MEM],
                                     e == 0, e == 1)
                st = 64 + 4 * (i % 4)
                neg_max, total = self.stat[:, st:st + 1], self.stat[:, st + 1:st + 2]
                self.DVE.wait(scores)
                maxed = self.reduce(neg_max, self.bank[b][:, 0:MEM], ALU.max, negate=True)
                self.ACT.wait(maxed, turned.get(i - 3))
                exped = self.act(ss[:, :], self.bank[b][:, 0:MEM], ACT.Exp, bias=neg_max, accum_out=total)
                self.bank_read[b] = [exped]
                self.DVE.wait(exped)
                inverse = self.reciprocal(total, total)
                self.DVE.wait(inverse)
                normed[i] = self.ts(ss[:, :], ss[:, :], total, ALU.mult)
            for _ in range(2):
                next(others, None)
            i = step - 1
            if 0 <= i < 4 * TB:
                hh, qb, bt, ss, p = i // TB, i % TB, 2 + i % 2, s[i % 3], pt[i // TB % 2]
                self.PE.wait(normed[i], self.bank_read[bt])
                for kb in range(2):
                    turned[i] = self.transpose(self.bank[bt][:, kb * P:(kb + 1) * P], ss[:, kb * P:(kb + 1) * P])
                to = p[:, :].rearrange("p (k q) -> p k q", k=2)[:, :, qb * P:(qb + 1) * P]
                self.ACT.wait(turned[i], pv_done.get(hh - 2))
                kept[i] = self.act(to, self.bank[bt][:, 0:MEM].rearrange("p (k q) -> p k q", k=2), ACT.Copy)
                self.bank_read[bt] = [kept[i]]
            for _ in range(2):
                next(others, None)
            i = step - 2
            if i >= 0 and i % TB == TB - 1:
                hh = i // TB
                p = pt[hh % 2]
                for e in range(2):
                    b, t, o = 4 + e, self.tmp[e], slice((2 * hh + e) * T, (2 * hh + e + 1) * T)
                    self.PE.wait(kept[i], self.bank_read[b])
                    for kb in range(2):
                        ov = kb * D + hh * 256 + e * P
                        product = self.mm(self.bank[b][:, :], v[:, ov:ov + P], p[:, kb * T:(kb + 1) * T], kb == 0, kb == 1)
                    self.ACT.wait(product, tmp_read[e])
                    out = self.act(t[:, :], self.bank[b][:, :], ACT.Copy)
                    self.bank_read[b] = [out]
                    self.ACT.wait(out)
                    cat_made[2 * hh + e] = self.split(t[:, :], chi[:, o], clo[:, o])
                    tmp_read[e] = cat_made[2 * hh + e][1]
                pv_done[hh] = product
        y = self.nc.alloc_sbuf_tensor_at("xa_y", [P, KT * T], F32, offset=self.at_big)
        self.seed_sums(0)
        reads = {}
        self.ACT.wait(tmp_read)
        self.out_proj([chi, clo], 8, self.proj_keep(y, reads), ready_k=cat_made)
        return y, reads["sum3"]

    def build(self):
        nc, g = self.nc, self.g
        x_loaded = []
        for n in range(4):
            if n == 1:
                self.load(self.consts[:, :], self.dram["c"], "const")
                loaded = self.load(self.par1[:, :], self.dram["p1"], "const")
            o = slice(n * 2 * T, (n + 1) * 2 * T)
            x_loaded += [self.load(self.x[:, o], self.dram["x"][:, o], f"x{n}")] * 2
        for n in range(2):
            self.DVE.do(lambda n=n: nc.vector.memset(self.stat[:, 158 + n:159 + n], 0.0), sem="gated")
        for e in (self.PE, self.DVE, self.POOL):
            e.wait(loaded)
        summed = self.squares_of_x(x_loaded)
        self.ACT.wait(loaded)
        self.DVE.wait(x_loaded)
        self.split_next_chunk(0, None)
        self.split_next_chunk(1, None)

        h_parts = self.norm_to_h(0, 1, summed, lambda k: self.p1("norm_mix", k))
        summed = self.mixer_one(h_parts)
        self.barrier()
        h_parts = self.norm_to_h(0, 1, summed, lambda k: self.p1("norm_ffn", k))
        summed = self.feed_forward(h_parts, self.ff_residual)
        rows = self.rstd_rows(0, 1, summed)
        self.DVE.wait(rows)
        normed = []
        for k in range(KT):
            xs = self.x[:, k * T:(k + 1) * T]
            normed.append(self.stt(xs, xs, self.p1("norm_final", k), self.bank[1][:, :], ALU.mult, ALU.mult))
        self.bank_read[1] = [normed[-1]]
        summed = self.squares_of_x(normed)
        self.barrier()

        with g.loop(LAYERS) as layer:
            for e in g.engines:
                e.wait([layer.before("end_" + other.name) for other in g.engines])
            loaded = self.load(self.par2[:, :], lambda: self.dram["p2"][bass.ds(layer.var * P, P), :], "par")
            self.DVE.wait(loaded)
            self.y = self.alias_h("ff_y", 0, KT * T)
            h_parts = self.norm_to_h(0, 1, None, lambda k: self.p2("ffn1_pre_g", k))
            summed = self.feed_forward(h_parts, self.ff_keep)
            summed = self.post_norm(lambda k: self.p2("ffn1_post_g", k), 0.5, self.y, summed)
            self.barrier()

            h_parts = self.norm_to_h(0, 1, summed, lambda k: self.p2("mix_pre_g", k))
            y, summed = self.mixer_two(h_parts)
            summed = self.post_norm(lambda k: self.p2("mix_post_g", k), 1.0, y, summed)
            self.barrier()

            h_parts = self.norm_to_h(0, 1, summed, lambda k: self.p2("xa_pre_g", k))
            y, summed = self.memory_attention(h_parts)
            summed = self.post_norm(lambda k: self.p2("xa_post_g", k), 1.0, y, summed)
            self.barrier()

            h_parts = self.norm_to_h(0, 1, summed, lambda k: self.p2("ffn2_pre_g", k))
            summed = self.feed_forward(h_parts, self.ff_keep)
            self.post_norm(lambda k: self.p2("ffn2_post_g", k), 0.5, self.y, summed)
            for e in g.engines:
                layer.names["end_" + e.name] = e.latest
        g.emit()

        w, count = self.dram["w"], self.dram["w"].shape[0]
        raw = [g.sem("raw0"), g.sem("raw1")]
        for s in range(2):
            nc.sync.dma_start(self.raw[s][:, :], w[s]).then_inc(raw[s], 16)
        with nc.sync.Fori(0, count // 2 - 1) as i:
            for s in range(2):
                nc.sync.wait_ge(g.sem("lo"), i * 2 + (s + 1))
                nc.sync.dma_start(self.raw[s][:, :], w[bass.ds(i * 2 + (2 + s), 1), :, :].rearrange("a p c -> (a p) c")).then_inc(raw[s], 16)
        nc.sync.wait_ge(g.sem("dve"), g.final["dve"])
        stored = g.sem("out")
        nc.sync.dma_start(self.dram["out"], self.x[:, :]).then_inc(stored, 16)
        nc.sync.wait_ge(stored, 16)


def build_program(nc, *args):
    k = Kernel(nc, *args)
    k.build()
    return k


def lay_out(i):
    a = {k: np.asarray(v) for k, v in i.items()}
    chunks = []

    def pad(rows):
        c = np.zeros((P, CHUNK), np.float32)
        c[:, :rows.shape[1]] = rows
        chunks.append(c)

    def cols(w, c0, n=256, k0=0, nk=KT):
        s = w[k0 * P:(k0 + nk) * P, c0:c0 + n].reshape(nk, P, n).transpose(1, 0, 2)
        t = np.zeros((P, nk, 256), np.float32)
        t[:, :, :n] = s
        pad(t.reshape(P, nk * 256))

    def ffn(wg, wu, wd):
        for f in range(FPAIR):
            cols(wg, f * 256)
            cols(wu, f * 256)
        for pair in range(4):
            for k0, nk in ((0, 8), (8, 8), (16, 6)):
                cols(wd, pair * 256, 256, k0, nk)

    w = a["w_in"][0]
    for c in range(0, 3072, 256):
        cols(w, c)
    for c in range(2):
        cols(w, 3080 + c * 256)
        cols(w, 3592 + c * 256)
    for pair in range(4):
        cols(a["w_out"][0], pair * 256, 256, 0, 8)
        cols(a["w_out"][0], pair * 256, 256, 8, 4)
    ffn(a["w_gate"][0], a["w_up"][0], a["w_down"][0])
    n1 = len(chunks)
    for l in range(LAYERS):
        ffn(a["ffn1_w_gate_2"][l], a["ffn1_w_up_2"][l], a["ffn1_w_down_2"][l])
        w = a["w_in_2"][l]
        for c in range(0, 1280, 256):
            cols(w, c)
        cols(w, 1280, 24)
        for kv in range(2):
            for part in range(2):
                cols(a["cmp_w1_2"][l, kv], 0, 256, part * 8, 8)
        for c in range(1304, 3352, 256):
            cols(w, c)
        for n in ("xa_wk_2", "xa_wv_2", "w_out_2", "xa_wq_2", "xa_wo_2"):
            for pair in range(4):
                cols(a[n][l], pair * 256)
        ffn(a["ffn2_w_gate_2"][l], a["ffn2_w_up_2"][l], a["ffn2_w_down_2"][l])
    assert n1 % 2 == 0 and len(chunks) % 2 == 0, (n1, len(chunks))
    chunks += [np.zeros((P, CHUNK), np.float32)] * 2

    def vec(v):
        return v.reshape(-1, P).T

    par1 = np.zeros((P, NPAR1), np.float32)
    for name, v in (("norm_mix", vec(a["norm_mix"][0])), ("norm_ffn", vec(a["norm_ffn"][0])),
                    ("ssd_conv_w", np.concatenate([vec(r) for r in a["ssd_conv_w"][0]], 1)),
                    ("ssd_conv_b", vec(a["ssd_conv_b"][0])), ("dt_bias", np.broadcast_to(a["ssd_dt_bias"][0], (P, 8))),
                    ("a_log", np.broadcast_to(a["ssd_a_log"][0], (P, 8))), ("d", np.broadcast_to(a["ssd_d"][0], (P, 8))),
                    ("ssd_norm", vec(a["ssd_norm"][0])), ("lru_conv_w", np.concatenate([vec(r) for r in a["lru_conv_w"][0]], 1)),
                    ("lru_conv_b", vec(a["lru_conv_b"][0])), ("lru_ba", vec(a["lru_ba"][0])), ("lru_bx", vec(a["lru_bx"][0])),
                    ("lru_lambda", vec(a["lru_lambda"][0])), ("norm_final", vec(a["norm_final"]))):
        o, n = PAR1[name]
        par1[:, o:o + n] = v
    lw = np.zeros((P, 1024 + 64), np.float32)
    for n, name in enumerate(("lru_wa", "lru_wx")):
        for b in range(8):
            r = (b % 2) * 64
            lw[r:r + 64, n * 512 + (b // 2) * P + r:n * 512 + (b // 2) * P + r + 64] = a[name][0, b]
    lw[:, 1024:] = a["w_in"][0][:, 3072:3080].reshape(KT, P, 8).transpose(1, 0, 2).reshape(P, 64)
    par2 = np.zeros((LAYERS * P, NPAR2), np.float32)
    for l in range(LAYERS):
        q = par2[l * P:(l + 1) * P]
        for name in ("ffn1_pre_g", "ffn1_post_g", "mix_pre_g", "mix_post_g", "xa_pre_g", "xa_mem_g", "xa_post_g",
                     "ffn2_pre_g", "ffn2_post_g", "nsa_out_g", "ret_gn_g"):
            o, n = PAR2[name]
            q[:, o:o + n] = vec(a[name + "_2"][l])
        o, n = PAR2["cmp_pe"]
        q[:, o:o + n] = a["cmp_pe_2"][l].reshape(2, 16, P).transpose(2, 0, 1).reshape(P, 32)
        o, n = PAR2["cmp_w2k"]
        wk = a["cmp_w2_2"][l, 0].reshape(2, P, 64).transpose(1, 0, 2)
        q[:, o:o + n] = np.concatenate([wk, wk], 2).reshape(P, 256)
        o, n = PAR2["cmp_w2v"]
        q[:, o:o + n] = a["cmp_w2_2"][l, 1].reshape(2, P, 64).transpose(1, 0, 2).reshape(P, 128)

    def feature_major(x, n):
        return np.ascontiguousarray(x.reshape(n, KT, P).transpose(2, 1, 0).reshape(P, KT * n))
    return dict(wstream=np.stack(chunks), xT=feature_major(a["x"][0], T), memT=feature_major(a["mem_2"][0], MEM),
                consts=CONSTS, par1=par1, lru_w=lw, par2=par2)


def kernel(**inputs):
    import concourse.bacc as bacc
    from concourse.bass_utils import run_bass_kernel_spmd

    nc = bacc.Bacc("TRN2", target_bir_lowering=False, num_devices=1)
    arrays = lay_out(inputs)
    args = [nc.dram_tensor(name, a.shape, mybir.dt.from_np(a.dtype), kind="ExternalInput").ap() for name, a in arrays.items()]
    args.append(nc.dram_tensor("outT", (P, KT * T), F32, kind="ExternalOutput").ap())
    build_program(nc, *args)
    r = run_bass_kernel_spmd(nc, [arrays], core_ids=[0])
    out = r.results[0]["outT"]
    return np.ascontiguousarray(out.reshape(P, KT, T).transpose(2, 1, 0).reshape(1, T, D))
```
